# Optimizing a Trainium2 kernel written in Bass

```python
import math
import jax, jax.numpy as jnp
from jax import lax
import numpy as np

D_MODEL = 1024
BATCH = 1
SEQ = 256
DEPTH = 2

N_A_LAYERS = DEPTH // 2
N_B_LAYERS = DEPTH - N_A_LAYERS
MIX_W = D_MODEL
MEM_LEN = 256
MEM_HEADS = 4
MEM_HEAD_DIM = 64
MEM_W = MEM_HEADS * MEM_HEAD_DIM
SEQ_MIX_W = MIX_W - MEM_W
HGRN_EXPAND = 128
HGRN_HEADS = SEQ_MIX_W // HGRN_EXPAND
HGRN_DK = HGRN_EXPAND
HGRN_DV = SEQ_MIX_W // HGRN_HEADS
HGRN_CHUNK = 64
SB_HEAD_DIM = 64
SB_HEADS = SEQ_MIX_W // SB_HEAD_DIM
SB_BLOCK = 128
A_IN_W = 4 * SEQ_MIX_W + MEM_W
B_IN_W = SEQ_MIX_W + MEM_W
N_GROUPS = 4
EXPERTS_PER_GROUP = 4
N_EXPERTS = N_GROUPS * EXPERTS_PER_GROUP
TOP_K_IN_GROUP = 2
D_EXPERT = 256
DEEPNORM_ALPHA = (2 * DEPTH) ** 0.25
DEEPNORM_BETA = (8 * DEPTH) ** -0.25
LN_EPS = 1e-5
RMS_EPS = 1e-6


def layer_norm(x, g, b):
    xf = x.astype(jnp.float32)
    mu = jnp.mean(xf, axis=-1, keepdims=True)
    var = jnp.mean(jnp.square(xf - mu), axis=-1, keepdims=True)
    y = (xf - mu) * lax.rsqrt(var + LN_EPS) * g.astype(jnp.float32) + b.astype(jnp.float32)
    return y.astype(x.dtype)

def post_norm(x, y, g, b):
    return layer_norm(DEEPNORM_ALPHA * x + y.astype(x.dtype), g, b)

def gla_chunkwise(q, k, v, logf):
    B, S, H, dk = q.shape
    dv = v.shape[-1]
    nc = S // HGRN_CHUNK

    def to_chunks(t):
        return t.reshape(B, nc, HGRN_CHUNK, H, t.shape[-1]).transpose(1, 0, 3, 2, 4)

    qc, kc, vc = to_chunks(q), to_chunks(k), to_chunks(v)
    G = jnp.cumsum(to_chunks(logf), axis=3)
    incl = jnp.tril(jnp.ones((HGRN_CHUNK, HGRN_CHUNK), dtype=bool))

    def step(state, inp):
        q_, k_, v_, G_ = inp
        diff = G_[:, :, :, None, :] - G_[:, :, None, :, :]
        decay = jnp.exp(jnp.where(incl[:, :, None], diff, -jnp.inf))
        scores = jnp.einsum('bhtd,bhsd,bhtsd->bhts', q_, k_, decay)
        out = (jnp.einsum('bhts,bhse->bhte', scores, v_)
               + jnp.einsum('bhtd,bhde->bhte', q_ * jnp.exp(G_), state))
        g_last = G_[:, :, -1]
        state = (jnp.exp(g_last)[..., None] * state
                 + jnp.einsum('bhsd,bhse->bhde', k_ * jnp.exp(g_last[:, :, None] - G_), v_))
        return state, out

    s0 = jnp.zeros((B, H, dk, dv), jnp.float32)
    _, out = lax.scan(step, s0, (qc, kc, vc, G))
    return out.transpose(1, 0, 3, 2, 4).reshape(B, S, H, dv)

def hgrn2_mix(q, f_raw, i_in, g, lb, gnorm):
    B, S, _ = q.shape
    qh = (jax.nn.silu(q.astype(jnp.float32)) * HGRN_DK ** -0.5).reshape(B, S, HGRN_HEADS, HGRN_DK)
    lbf = lb.astype(jnp.float32)
    logf = jnp.logaddexp(jnp.log(lbf), jnp.log1p(-lbf) + jax.nn.log_sigmoid(f_raw.astype(jnp.float32)))
    logf = logf.reshape(B, S, HGRN_HEADS, HGRN_DK)
    kh = -jnp.expm1(logf)
    vh = i_in.astype(jnp.float32).reshape(B, S, HGRN_HEADS, HGRN_DV)
    o = gla_chunkwise(qh, kh, vh, logf)
    o = o * lax.rsqrt(jnp.mean(jnp.square(o), axis=-1, keepdims=True) + RMS_EPS)
    o = o * gnorm.astype(jnp.float32).reshape(HGRN_HEADS, HGRN_DV)
    o = o.reshape(B, S, SEQ_MIX_W) * jax.nn.silu(g.astype(jnp.float32))
    return o

def stick_breaking_attention(q, k, v):
    B, S, _ = q.shape
    qh = q.astype(jnp.float32).reshape(B, S, SB_HEADS, SB_HEAD_DIM).transpose(0, 2, 1, 3)
    scale = 1.0 / math.sqrt(SB_HEAD_DIM)
    outs = []
    for blk in range(S // SB_BLOCK):
        start, end = blk * SB_BLOCK, (blk + 1) * SB_BLOCK
        qb = qh[:, :, start:end]
        kb, vb = k[:, :, :end], v[:, :, :end]
        z = jnp.einsum('bhtd,bhsd->bhts', qb, kb) * scale
        t_pos = start + jnp.arange(SB_BLOCK)
        s_pos = jnp.arange(end)
        mask = s_pos[None, :] < t_pos[:, None]
        neg_log_1m_beta = jnp.where(mask, jax.nn.softplus(z), 0.0)
        rest = lax.cumsum(neg_log_1m_beta, axis=3, reverse=True) - neg_log_1m_beta
        log_a = jax.nn.log_sigmoid(z) - rest
        a = jnp.where(mask, jnp.exp(log_a), 0.0)
        outs.append(jnp.einsum('bhts,bhsd->bhtd', a, vb))
    o = jnp.concatenate(outs, axis=2)
    return o.transpose(0, 2, 1, 3).reshape(B, S, SEQ_MIX_W)

def memory_attention(qm, mem_k, mem_v):
    B, S, _ = qm.shape
    qh = qm.astype(jnp.float32).reshape(B, S, MEM_HEADS, MEM_HEAD_DIM)
    scores = jnp.einsum('bthd,bmhd->bhtm', qh, mem_k.astype(jnp.float32)) / math.sqrt(MEM_HEAD_DIM)
    p = jax.nn.softmax(scores, axis=-1)
    o = jnp.einsum('bhtm,bmhd->bthd', p, mem_v.astype(jnp.float32))
    return o.reshape(B, S, MEM_W)

def hier_moe(x, w_group, b_group, w_router, b_router, w_gate, w_up, w_down):
    B, S, D = x.shape
    xf = x.reshape(B * S, D)
    T = xf.shape[0]
    probs_g = jax.nn.softmax((xf @ w_group + b_group).astype(jnp.float32), axis=-1)
    p_top, g_idx = lax.top_k(probs_g, 1)
    logits_e = (xf @ w_router + b_router).astype(jnp.float32).reshape(T, N_GROUPS, EXPERTS_PER_GROUP)
    in_group = jnp.take_along_axis(logits_e, g_idx[:, :, None], axis=1)[:, 0]
    probs_in = jax.nn.softmax(in_group, axis=-1)
    w_top, e_local = lax.top_k(probs_in, TOP_K_IN_GROUP)
    w_top = w_top / jnp.sum(w_top, axis=-1, keepdims=True)
    ids = g_idx * EXPERTS_PER_GROUP + e_local
    gates = jnp.einsum('tk,tke->te', p_top * w_top, jax.nn.one_hot(ids, N_EXPERTS, dtype=jnp.float32))
    h = jax.nn.silu(jnp.einsum('td,edf->tef', xf, w_gate)) * jnp.einsum('td,edf->tef', xf, w_up)
    y = jnp.einsum('tef,efd->td', h * gates[:, :, None].astype(h.dtype), w_down)
    return y.reshape(B, S, D)

def first_inputs(seed: int = 0) -> dict:
    key = jax.random.key(seed)
    ks = iter(jax.random.split(key, 40))

    def nrm(shape, scale):
        return jax.random.normal(next(ks), shape, jnp.float32) * scale

    d_s = D_MODEL ** -0.5
    x = nrm((BATCH, SEQ, D_MODEL), 1.0)
    mem = nrm((BATCH, MEM_LEN, D_MODEL), 1.0)
    a_w_in = jnp.concatenate([
        nrm((N_A_LAYERS, D_MODEL, SEQ_MIX_W), d_s),
        nrm((N_A_LAYERS, D_MODEL, SEQ_MIX_W), d_s),
        nrm((N_A_LAYERS, D_MODEL, SEQ_MIX_W), d_s * DEEPNORM_BETA),
        nrm((N_A_LAYERS, D_MODEL, SEQ_MIX_W), d_s),
        nrm((N_A_LAYERS, D_MODEL, MEM_W), d_s),
    ], axis=-1)
    a_lower_bounds = nrm((N_A_LAYERS, SEQ_MIX_W), 0.1)
    a_gnorm = 1.0 + nrm((N_A_LAYERS, SEQ_MIX_W), 0.02)
    b_w_in = nrm((N_B_LAYERS, D_MODEL, B_IN_W), d_s)
    w_kv_shared = jnp.concatenate([nrm((D_MODEL, SEQ_MIX_W), d_s),
                                   nrm((D_MODEL, SEQ_MIX_W), d_s * DEEPNORM_BETA)], axis=-1)
    w_mem_kv = jnp.concatenate([nrm((DEPTH, D_MODEL, MEM_W), d_s),
                                nrm((DEPTH, D_MODEL, MEM_W), d_s * DEEPNORM_BETA)], axis=-1)
    w_o = nrm((DEPTH, MIX_W, D_MODEL), MIX_W ** -0.5 * DEEPNORM_BETA)
    ln_mix_g = 1.0 + nrm((DEPTH, D_MODEL), 0.02)
    ln_mix_b = nrm((DEPTH, D_MODEL), 0.02)
    ln_ffn_g = 1.0 + nrm((DEPTH, D_MODEL), 0.02)
    ln_ffn_b = nrm((DEPTH, D_MODEL), 0.02)
    w_group = nrm((DEPTH, D_MODEL, N_GROUPS), d_s)
    b_group = nrm((DEPTH, N_GROUPS), 0.01)
    w_router = nrm((DEPTH, D_MODEL, N_EXPERTS), d_s)
    b_router = nrm((DEPTH, N_EXPERTS), 0.01)
    w_gate = nrm((DEPTH, N_EXPERTS, D_MODEL, D_EXPERT), d_s)
    w_up = nrm((DEPTH, N_EXPERTS, D_MODEL, D_EXPERT), d_s)
    w_down = nrm((DEPTH, N_EXPERTS, D_EXPERT, D_MODEL), D_EXPERT ** -0.5 * DEEPNORM_BETA)
    return {"x": x, "mem": mem, "a_w_in": a_w_in, "a_lower_bounds": a_lower_bounds,
            "a_gnorm": a_gnorm, "b_w_in": b_w_in, "w_kv_shared": w_kv_shared,
            "w_mem_kv": w_mem_kv, "w_o": w_o, "ln_mix_g": ln_mix_g, "ln_mix_b": ln_mix_b,
            "ln_ffn_g": ln_ffn_g, "ln_ffn_b": ln_ffn_b, "w_group": w_group, "b_group": b_group,
            "w_router": w_router, "b_router": b_router, "w_gate": w_gate, "w_up": w_up,
            "w_down": w_down}

def first_block(x, mem, a_w_in, a_lower_bounds, a_gnorm, b_w_in, w_kv_shared, w_mem_kv, w_o,
              ln_mix_g, ln_mix_b, ln_ffn_g, ln_ffn_b, w_group, b_group, w_router, b_router,
              w_gate, w_up, w_down):
    B, S, _ = x.shape
    lb_all = jnp.cumsum(jax.nn.softmax(a_lower_bounds.astype(jnp.float32), axis=0), axis=0)
    lb_all = lb_all - lb_all[0]
    shared_k = None
    shared_v = None
    for layer in range(DEPTH):
        mem_kv = mem @ w_mem_kv[layer]
        mem_k = mem_kv[..., :MEM_W].reshape(B, MEM_LEN, MEM_HEADS, MEM_HEAD_DIM)
        mem_v = mem_kv[..., MEM_W:].reshape(B, MEM_LEN, MEM_HEADS, MEM_HEAD_DIM)
        if layer < N_A_LAYERS:
            h = x @ a_w_in[layer]
            q, f_raw, i_in, g, qm = jnp.split(
                h, [SEQ_MIX_W, 2 * SEQ_MIX_W, 3 * SEQ_MIX_W, 4 * SEQ_MIX_W], axis=-1)
            seq_out = hgrn2_mix(q, f_raw, i_in, g, lb_all[layer], a_gnorm[layer])
        else:
            if layer == N_A_LAYERS:
                kv = x @ w_kv_shared
                shared_k = kv[..., :SEQ_MIX_W].astype(jnp.float32).reshape(
                    B, S, SB_HEADS, SB_HEAD_DIM).transpose(0, 2, 1, 3)
                shared_v = kv[..., SEQ_MIX_W:].astype(jnp.float32).reshape(
                    B, S, SB_HEADS, SB_HEAD_DIM).transpose(0, 2, 1, 3)
            h = x @ b_w_in[layer - N_A_LAYERS]
            q, qm = jnp.split(h, [SEQ_MIX_W], axis=-1)
            seq_out = stick_breaking_attention(q, shared_k, shared_v)
        mem_out = memory_attention(qm, mem_k, mem_v)
        mixed = jnp.concatenate([seq_out.astype(x.dtype), mem_out.astype(x.dtype)], axis=-1)
        x = post_norm(x, mixed @ w_o[layer], ln_mix_g[layer], ln_mix_b[layer])
        moe_out = hier_moe(x, w_group[layer], b_group[layer], w_router[layer], b_router[layer],
                           w_gate[layer], w_up[layer], w_down[layer])
        x = post_norm(x, moe_out, ln_ffn_g[layer], ln_ffn_b[layer])
    return x


MLA_HEADS = 8
QK_NOPE_DIM = 64
QK_ROPE_DIM = 32
V_HEAD_DIM = 64
Q_LORA_RANK = 384
KV_LORA_RANK = 256
ROPE_THETA = 10000.0
Q_BLOCK = 128
SG_GROUPS = 8
SG_GROUP_DIM = 64
SG_WIDTH = SG_GROUPS * SG_GROUP_DIM
SG_CHUNK = 128
CONV_WIDTH = D_MODEL
CONV_K = 3
D_FF = 2816
NORM_EPS = 1e-6

MLA_OUT = MLA_HEADS * V_HEAD_DIM
MIX_WIDTH = MLA_OUT + SG_WIDTH
QK_HEAD_DIM = QK_NOPE_DIM + QK_ROPE_DIM
EVEN_IN = Q_LORA_RANK + KV_LORA_RANK + QK_ROPE_DIM + 2 * SG_WIDTH
N_EVEN = (DEPTH + 1) // 2
N_ODD = DEPTH // 2


def rms_norm(x, g):
    x32 = x.astype(jnp.float32)
    y = x32 * lax.rsqrt(jnp.mean(x32 * x32, axis=-1, keepdims=True) + NORM_EPS)
    return (y * g.astype(jnp.float32)).astype(x.dtype)

def swiglu(h, w_gate, w_up, w_down):
    return (jax.nn.silu(h @ w_gate) * (h @ w_up)) @ w_down

def rope_tables(positions):
    inv_freq = ROPE_THETA ** (-jnp.arange(0, QK_ROPE_DIM, 2, dtype=jnp.float32) / QK_ROPE_DIM)
    ang = positions.astype(jnp.float32)[..., None] * inv_freq
    return jnp.cos(ang), jnp.sin(ang)

def apply_rope(t, cos, sin):
    t32 = t.astype(jnp.float32)
    t1, t2 = jnp.split(t32, 2, axis=-1)
    out = jnp.concatenate([t1 * cos - t2 * sin, t1 * sin + t2 * cos], axis=-1)
    return out.astype(t.dtype)

def mla_attention(q_nope, q_rope, k_nope, k_rope, v):
    B, S, H, _ = q_nope.shape
    nb = S // Q_BLOCK
    scale = QK_HEAD_DIM ** -0.5
    k_idx = jnp.arange(S)

    def to_blocks(t):
        return jnp.moveaxis(t.reshape(B, nb, Q_BLOCK, *t.shape[2:]), 1, 0)

    def one_block(args):
        qn, qr, i = args
        s = (jnp.einsum('bqhd,bkhd->bhqk', qn, k_nope, preferred_element_type=jnp.float32)
             + jnp.einsum('bqhr,bkr->bhqk', qr, k_rope, preferred_element_type=jnp.float32)) * scale
        q_idx = i * Q_BLOCK + jnp.arange(Q_BLOCK)
        s = jnp.where(k_idx[None, :] <= q_idx[:, None], s, -jnp.inf)
        p = jax.nn.softmax(s, axis=-1).astype(v.dtype)
        return jnp.einsum('bhqk,bkhd->bqhd', p, v)

    out = lax.map(one_block, (to_blocks(q_nope), to_blocks(q_rope), jnp.arange(nb)))
    return jnp.moveaxis(out, 0, 1).reshape(B, S, H * V_HEAD_DIM)

def spatial_gating(z, sg_norm, sg_w, sg_b):
    u, v = jnp.split(z, 2, axis=-1)
    v = rms_norm(v, sg_norm)
    B, S, _ = v.shape
    nc = S // SG_CHUNK
    v = v.reshape(B, nc, SG_CHUNK, SG_GROUPS, SG_GROUP_DIM)
    w = sg_w * jnp.tril(jnp.ones((SG_CHUNK, SG_CHUNK), dtype=sg_w.dtype))
    mixed = jnp.einsum('gts,bnsgc->bntgc', w, v) + sg_b.T[None, None, :, :, None]
    return u * mixed.reshape(B, S, SG_WIDTH)

def mla_sgu_mixer(h, cos, sin, w_in, q_norm, w_uq, kv_norm, w_ukv, sg_norm, sg_w, sg_b, w_out):
    B, S, _ = h.shape
    proj = h @ w_in
    c_q, c_kv, k_rope, z = jnp.split(
        proj, [Q_LORA_RANK, Q_LORA_RANK + KV_LORA_RANK, Q_LORA_RANK + KV_LORA_RANK + QK_ROPE_DIM], axis=-1)
    q = (rms_norm(c_q, q_norm) @ w_uq).reshape(B, S, MLA_HEADS, QK_HEAD_DIM)
    q_nope = q[..., :QK_NOPE_DIM]
    q_rope = apply_rope(q[..., QK_NOPE_DIM:], cos[:, :, None, :], sin[:, :, None, :])
    k_rope = apply_rope(k_rope, cos, sin)
    kv = (rms_norm(c_kv, kv_norm) @ w_ukv).reshape(B, S, MLA_HEADS, QK_NOPE_DIM + V_HEAD_DIM)
    k_nope, v = kv[..., :QK_NOPE_DIM], kv[..., QK_NOPE_DIM:]
    attn = mla_attention(q_nope, q_rope, k_nope, k_rope, v)
    sg = spatial_gating(jax.nn.gelu(z, approximate=False), sg_norm, sg_w, sg_b)
    return jnp.concatenate([attn, sg], axis=-1) @ w_out

def short_conv_mixer(h, w_in, conv_w, w_out):
    b_gate, c_gate, z = jnp.split(h @ w_in, 3, axis=-1)
    y = lax.conv_general_dilated(
        c_gate * z, conv_w[:, None, :], window_strides=(1,), padding=[(CONV_K - 1, 0)],
        dimension_numbers=('NWC', 'WIO', 'NWC'), feature_group_count=CONV_WIDTH)
    return (b_gate * y) @ w_out

def second_inputs(seed: int = 0) -> dict:
    key = jax.random.key(seed)
    keys = iter(jax.random.split(key, 32))
    f32 = jnp.float32

    def dense(shape, fan_in):
        return jax.random.normal(next(keys), shape, f32) * (fan_in ** -0.5)

    def gain(shape):
        return 1.0 + 0.1 * jax.random.normal(next(keys), shape, f32)

    x = jax.random.normal(next(keys), (BATCH, SEQ, D_MODEL), f32)
    offset = jax.random.randint(next(keys), (BATCH, 1), 0, 1024, dtype=jnp.int32)
    positions = offset + jnp.arange(SEQ, dtype=jnp.int32)[None, :]
    return {
        "x": x,
        "positions": positions,
        "ffn_pre_norm": gain((DEPTH, D_MODEL)),
        "ffn_pre_w_gate": dense((DEPTH, D_MODEL, D_FF), D_MODEL),
        "ffn_pre_w_up": dense((DEPTH, D_MODEL, D_FF), D_MODEL),
        "ffn_pre_w_down": dense((DEPTH, D_FF, D_MODEL), D_FF),
        "mix_norm": gain((DEPTH, D_MODEL)),
        "ffn_post_norm": gain((DEPTH, D_MODEL)),
        "ffn_post_w_gate": dense((DEPTH, D_MODEL, D_FF), D_MODEL),
        "ffn_post_w_up": dense((DEPTH, D_MODEL, D_FF), D_MODEL),
        "ffn_post_w_down": dense((DEPTH, D_FF, D_MODEL), D_FF),
        "even_w_in": dense((N_EVEN, D_MODEL, EVEN_IN), D_MODEL),
        "q_norm": gain((N_EVEN, Q_LORA_RANK)),
        "w_uq": dense((N_EVEN, Q_LORA_RANK, MLA_HEADS * QK_HEAD_DIM), Q_LORA_RANK),
        "kv_norm": gain((N_EVEN, KV_LORA_RANK)),
        "w_ukv": dense((N_EVEN, KV_LORA_RANK, MLA_HEADS * (QK_NOPE_DIM + V_HEAD_DIM)), KV_LORA_RANK),
        "sg_norm": gain((N_EVEN, SG_WIDTH)),
        "sg_w": dense((N_EVEN, SG_GROUPS, SG_CHUNK, SG_CHUNK), SG_CHUNK),
        "sg_b": gain((N_EVEN, SG_GROUPS, SG_CHUNK)),
        "even_w_out": dense((N_EVEN, MIX_WIDTH, D_MODEL), MIX_WIDTH),
        "conv_w_in": dense((N_ODD, D_MODEL, 3 * CONV_WIDTH), D_MODEL),
        "conv_w": dense((N_ODD, CONV_K, CONV_WIDTH), CONV_K),
        "conv_w_out": dense((N_ODD, CONV_WIDTH, D_MODEL), CONV_WIDTH),
        "final_norm": gain((D_MODEL,)),
    }

def second_block(x, positions, ffn_pre_norm, ffn_pre_w_gate, ffn_pre_w_up, ffn_pre_w_down,
              mix_norm, ffn_post_norm, ffn_post_w_gate, ffn_post_w_up, ffn_post_w_down,
              even_w_in, q_norm, w_uq, kv_norm, w_ukv, sg_norm, sg_w, sg_b, even_w_out,
              conv_w_in, conv_w, conv_w_out, final_norm):
    cos, sin = rope_tables(positions)
    for layer in range(DEPTH):
        x = x + 0.5 * swiglu(rms_norm(x, ffn_pre_norm[layer]),
                             ffn_pre_w_gate[layer], ffn_pre_w_up[layer], ffn_pre_w_down[layer])
        h = rms_norm(x, mix_norm[layer])
        if layer % 2 == 0:
            e = layer // 2
            x = x + mla_sgu_mixer(h, cos, sin, even_w_in[e], q_norm[e], w_uq[e], kv_norm[e],
                                  w_ukv[e], sg_norm[e], sg_w[e], sg_b[e], even_w_out[e])
        else:
            o = layer // 2
            x = x + short_conv_mixer(h, conv_w_in[o], conv_w[o], conv_w_out[o])
        x = x + 0.5 * swiglu(rms_norm(x, ffn_post_norm[layer]),
                             ffn_post_w_gate[layer], ffn_post_w_up[layer], ffn_post_w_down[layer])
    return rms_norm(x, final_norm)


def setup_inputs(seed=0):
    out = dict(first_inputs(seed))
    for name, value in second_inputs(seed + 1).items():
        if name != "x":
            out[name + "_2"] = value
    return out


def reference(
    x, mem, a_w_in, a_lower_bounds, a_gnorm, b_w_in, w_kv_shared, w_mem_kv, w_o, ln_mix_g,
    ln_mix_b, ln_ffn_g, ln_ffn_b, w_group, b_group, w_router, b_router, w_gate, w_up, w_down,
    positions_2, ffn_pre_norm_2, ffn_pre_w_gate_2, ffn_pre_w_up_2, ffn_pre_w_down_2, mix_norm_2,
    ffn_post_norm_2, ffn_post_w_gate_2, ffn_post_w_up_2, ffn_post_w_down_2, even_w_in_2,
    q_norm_2, w_uq_2, kv_norm_2, w_ukv_2, sg_norm_2, sg_w_2, sg_b_2, even_w_out_2, conv_w_in_2,
    conv_w_2, conv_w_out_2, final_norm_2,
):
    x = first_block(
        x, mem, a_w_in, a_lower_bounds, a_gnorm, b_w_in, w_kv_shared, w_mem_kv, w_o, ln_mix_g,
        ln_mix_b, ln_ffn_g, ln_ffn_b, w_group, b_group, w_router, b_router, w_gate, w_up,
        w_down,
    )
    return second_block(
        x, positions_2, ffn_pre_norm_2, ffn_pre_w_gate_2, ffn_pre_w_up_2, ffn_pre_w_down_2,
        mix_norm_2, ffn_post_norm_2, ffn_post_w_gate_2, ffn_post_w_up_2, ffn_post_w_down_2,
        even_w_in_2, q_norm_2, w_uq_2, kv_norm_2, w_ukv_2, sg_norm_2, sg_w_2, sg_b_2,
        even_w_out_2, conv_w_in_2, conv_w_2, conv_w_out_2, final_norm_2,
    )


_drawn_inputs = setup_inputs


def setup_inputs(seed=0):
    import zlib

    import numpy as np

    out = dict(_drawn_inputs(seed))
    spreads = {}
    factors = {'a_gnorm': 6.047, 'b_group': 5.217, 'b_router': 8.0, 'q_norm_2': 3.668}
    for name, (base, spread) in spreads.items():
        noise = np.random.default_rng([zlib.crc32(name.encode()), seed]).standard_normal(out[name].shape)
        drawn = base * np.exp(spread * noise) if base else spread * noise
        out[name] = __import__('jax').numpy.asarray(drawn.astype(out[name].dtype))
    for name, factor in factors.items():
        out[name] = (out[name] * factor).astype(out[name].dtype)
    return out
```

```python
from contextlib import ExitStack

import numpy as np

import concourse.bass as bass
from concourse import mybir

F32 = mybir.dt.float32
F32R = mybir.dt.float32r
I32 = mybir.dt.int32
U8 = mybir.dt.uint8
ALU = mybir.AluOpType
ACT = mybir.ActivationFunctionType
AX = mybir.AxisListType.X

P = 128
D = 1024
S = 256
NT = S // P
KC = D // P
RING = 3
UNIT = 2048
UC = 256
HEADS_A, HEADS_B, HEADS_MEM, HEADS_MLA = 6, 12, 4, 8
EXPERTS, GROUPS = 16, 4
MIX = 768
D_FF = 2816
NOPE, ROPE, QKH = 64, 32, 96
ALPHA = 4 ** 0.25
LN_EPS, RMS_EPS = 1e-5, 1e-6
NEG = -1e30
LEVELS = [2, 4, 8, 16, 32, 64, 128]
STREAM_UNITS = (4 + 13 + 4) + 3 * EXPERTS + (6 + 4 + 4) + 3 * EXPERTS + 4 * 3 * (D_FF // UC) + (7 + 3 + 4 + 4) + (12 + 4)

EVEN_UNIT = 21 + 48 + 14 + 48 + 33


def unit_width(u):
    k = u - EVEN_UNIT
    return KC * 160 if k == 2 else 3 * UC if 7 <= k < 10 else 2 * UC if 10 <= k < 14 else UNIT


def build_kernel(nc, a, out):
    with ExitStack() as ctx:
        def sb(name, shape, dt=F32):
            return ctx.enter_context(nc.sbuf_tensor(name, shape, dt))

        def sem(name):
            return ctx.enter_context(nc.semaphore(name))

        RAW = sb("RAW", [P, RING, UNIT])
        HI = sb("HI", [P, RING, UNIT], F32R)
        LO = sb("LO", [P, RING, UNIT], F32R)
        X = sb("X", [P, NT, D])
        XN = sb("XN", [P, NT, D])
        XTH, XTL = (sb(n, [P, KC, S], F32R) for n in ("XTH", "XTL"))
        CTH, CTL = (sb(n, [P, KC, S], F32R) for n in ("CTH", "CTL"))
        MK = sb("MK", [P, 2, 2, S])
        MV = sb("MV", [P, 2, NT, S])
        SG, HT = sb("SG", [P, 2 * S]), sb("HT", [P, 2 * S])
        HH, HL = (sb(n, [P, 2, S], F32R) for n in ("HH", "HL"))
        IDENT, ONES = sb("IDENT", [P, P]), sb("ONES", [P, P])
        STRICT = sb("STRICT", [P, P])
        TRIL = sb("TRIL", [P, P])
        NSUF = sb("NSUF", [P, P])
        NONE = sb("NONE", [P, P])
        CAUS = sb("CAUS", [P, P])
        MSK = sb("MSK", [P, len(LEVELS) + 2, P], U8)
        MTMP = sb("MTMP", [P, P])
        W4 = sb("W4", [P, 4])
        POS, INVF = sb("POS", [P, NT], I32), sb("INVF", [P, ROPE // 2])
        COLS = sb("COLS", [P, 4])
        PV = sb("PV", [P, 160])
        PV2 = PV[:, 70:160]
        RWR = sb("RWR", [P, 2, KC, 20])
        RWH, RWL = (sb(n, [P, 2, KC, 20], F32R) for n in ("RWH", "RWL"))
        RB = sb("RB", [P, 2, 20])
        LNG, LNB = sb("LNG", [P, D]), sb("LNB", [P, D])
        ST = sb("ST", [P, NT, 16])
        SM = sb("SM", [P, 640])
        AR = sb("AR", [P, 13056])

        def ar(off, *shape):
            n = int(np.prod(shape))
            assert off + n <= 13056
            v = AR[:, off:off + n]
            names = "abcd"[:len(shape)]
            if len(shape) == 1:
                return v
            return v.rearrange(f"p ({' '.join(names)}) -> p {' '.join(names)}", **dict(zip(names, shape)))

        PB = ctx.enter_context(nc.psum_tensor("PB", [P, 4, 512], F32))
        Y = ctx.enter_context(nc.psum_tensor("Y", [P, NT, D], F32))

        gate_dram = nc.dram_tensor("gate_scratch", (2, EXPERTS, S), F32, kind="Internal").ap()

        raw_in = [sem(f"raw_in{i}") for i in range(RING)]
        p_free = [sem(f"p_free{i}") for i in range(4)]
        y_free = [sem(f"y_free{i}") for i in range(2)]
        names = """w_hi w_split w_used out_done x_in out_in mem_in par_in rw_in rb_in ln_in sgn_in fin_in sgw_in pos_in gt_out gb_in
        pool_const dve_chain act_chain pool_chain rw_ready
        tp_full tmp_d tp_hi x_sum sq_sum rw_hi
        n_act n_dve xn_ready x_ready
        f_act lf_done gs_ready g_ready dlow dhigh e_done m_low m_high lvl_full at_ready am_zero
        o_full sq_done ss_full rt_done ct_hi ct_lo o_norm q_ready
        sc_full mx_ready pe_done at_full ao_full 
        z_full sp_act sp_ready la_full ea_done am_ready so_full lmin
        rt_full r_dve r_act gt_ready gt_sb
        h_mul h_gb h_hi h_lo
        cq_act cq_done rope_cs rope_act q_ev qt_full sgw_tp vn_ready sgo_ready mix_full
        conv_done""".split()
        s = {n: sem(n) for n in names}

        def wT(w, r0, k, c0, n):
            return w[r0:r0 + k * P, c0:c0 + n].rearrange("(k p) n -> p k n", p=P)

        class Count:
            def __init__(self):
                self.u = 0
                self.v = 0
                self.uses = [0] * 4
                self.yuses = [0] * 2
                self.n = {}

            def next(self, name, k=1):
                self.n[name] = self.n.get(name, 0) + k
                return self.n[name]

            def at(self, name):
                return self.n.get(name, 0)

        block = ctx.enter_context(nc.Block())

        @block.sync
        def _(sp):
            n = Count()

            def load(src, k, cols, i=0):
                slot = n.u % RING
                if n.u >= RING or not isinstance(i, int):
                    sp.wait_ge(s["w_split"], n.u - RING + 1 + i * RING)
                dst = RAW[:, slot, 0:k * cols].rearrange("p (k n) -> p k n", k=k)
                sp.dma_start(dst, src).then_inc(raw_in[slot], 16)
                n.u += 1

            def load_cols(w, r0, k, c0, cols):
                load(wT(w, r0, k, c0, cols), k, cols)

            def load_rows(w):
                for r in range(4):
                    load(wT(w, r * UC, 2, 0, D), 2, D)

            def ffn(gate, up, down, chunks, peel):
                def body(j, i):
                    load(gate(i + j + 1), KC, UC, i)
                    load(up(i + j + 1), KC, UC, i)
                    load(down(i + j), 2, D, i)

                load(gate(0), KC, UC)
                load(up(0), KC, UC)
                body(0, 0)
                loops = chunks - 2 - peel
                u0 = n.u
                with sp.Fori(0, loops) as i:
                    body(1, i)
                n.u = u0 + RING * loops
                for j in range(1 + loops, chunks - 1):
                    body(j, 0)
                load(down(chunks - 1), 2, D)

            def moe(layer):
                def expert(w, k):
                    def at(e):
                        if isinstance(e, int):
                            return w[layer, e].rearrange("(k p) n -> p k n", p=P)
                        return w[layer, bass.ds(e, 1)].rearrange("e (k p) n -> p (e k) n", p=P)
                    return at
                ffn(expert(a["w_gate"], KC), expert(a["w_up"], KC), expert(a["w_down"], 2), EXPERTS, 0)

            def swiglu(g, u, d, layer, peel=0):
                def cols(w):
                    return lambda c: w[layer][:, bass.ds(c * UC, UC)].rearrange("(k p) n -> p k n", p=P)

                def rows(c):
                    return d[layer][bass.ds(c * UC, UC), :].rearrange("(k p) n -> p k n", p=P)
                ffn(cols(g), cols(u), rows, D_FF // UC, peel)

            for t in range(NT):
                sp.dma_start(XN[:, t, :], a["mem"][0, t * P:(t + 1) * P, :]).then_inc(s["mem_in"], 16)
            sp.dma_start(X[:, :, :], a["x"][0].rearrange("(t p) n -> p t n", p=P)).then_inc(s["x_in"], 16)
            load_cols(a["w_mem_kv"][0], 0, KC, 0, UC)
            load_cols(a["w_mem_kv"][0], 0, KC, UC, UC)
            for base in (MIX, 0, 2 * MIX):
                for j in range(3):
                    load_cols(a["a_w_in"][0], 0, KC, base + j * UC, UC)
            load_cols(a["a_w_in"][0], 0, KC, 4 * MIX, UC)
            for j in range(3):
                load_cols(a["a_w_in"][0], 0, KC, 3 * MIX + j * UC, UC)
            load_cols(a["w_mem_kv"][1], 0, KC, 0, UC)
            load_cols(a["w_mem_kv"][1], 0, KC, UC, UC)
            load_rows(a["w_o"][0])
            moe(0)
            for j in range(6):
                load_cols(a["w_kv_shared"], 0, KC, j * UC, UC)
            for j in range(4):
                load_cols(a["b_w_in"][0], 0, KC, j * UC, UC)
            load_rows(a["w_o"][1])
            moe(1)
            swiglu(a["ffn_pre_w_gate_2"], a["ffn_pre_w_up_2"], a["ffn_pre_w_down_2"], 0)
            w = a["even_w_in_2"][0]
            load_cols(w, 0, KC, 0, UC)
            load_cols(w, 0, KC, UC, UC)
            load_cols(w, 0, KC, 2 * UC, 160)
            for j in range(4):
                load_cols(w, 0, KC, 672 + j * UC, UC)
            for j in range(3):
                load_cols(a["w_uq_2"][0], 0, 3, j * UC, UC)
            for j in range(4):
                load_cols(a["w_ukv_2"][0], 0, 2, j * UC, UC)
            load_rows(a["even_w_out_2"][0])
            swiglu(a["ffn_post_w_gate_2"], a["ffn_post_w_up_2"], a["ffn_post_w_down_2"], 0)
            swiglu(a["ffn_pre_w_gate_2"], a["ffn_pre_w_up_2"], a["ffn_pre_w_down_2"], 1)
            for j in range(4):
                for part in (1, 2, 0):
                    load_cols(a["conv_w_in_2"][0], 0, KC, part * D + j * UC, UC)
            load_rows(a["conv_w_out_2"][0])
            swiglu(a["ffn_post_w_gate_2"], a["ffn_post_w_up_2"], a["ffn_post_w_down_2"], 1, peel=1)
            assert n.u == STREAM_UNITS, (n.u, STREAM_UNITS)
            for t in range(NT):
                sp.wait_ge(s["out_in"], t + 1)
                sp.dma_start(out[0, t * P:(t + 1) * P, :], XN[:, t, :]).then_inc(s["out_done"], 16)
            sp.wait_ge(s["out_done"], 16 * NT)

        G, KK, Q, GS = ar(0, 1536), ar(1536, 1536), ar(3072, 1536), ar(6144, 1536)
        V0 = ar(4608, NT, MIX)
        MB = [ar(7680, 1536), ar(9216, 1536)]
        ATD, ATX = ar(10752, 12, P), ar(12288, 6, P)
        QM0 = XN[:, 0, 0:2 * S].rearrange("p (a b) -> p a b", a=2)
        PN0, PT0 = ar(7680, 4, NT, S), ar(1536, 4, 2, S)
        QB, KB, VB = ar(0, 6, S), ar(1536, 6, S), ar(3072, NT, MIX)
        QM1 = ar(4608, 2, S)
        SBW = [[ar(5120 + 1536 * z + 384 * k, 384) for k in range(4)] for z in range(2)]
        PN1, PT1 = ar(8192, 4, NT, S), ar(10240, 4, 2, S)
        GB = ar(0, EXPERTS, S)
        QT, KT = ar(0, HEADS_MLA, S), ar(2048, HEADS_MLA, S)
        VV = ar(4096, NT, 512)
        PRJ = ar(5120, NT, 672)
        QN, KF = ar(6464, NT, MIX), ar(8000, NT, MIX)
        ZG = ar(9536, NT, D)
        SGWT = ar(11584, 8, P)
        SGW = ar(8000, 8, P)
        PN2, PT2 = ar(5120, 4, NT, S), ar(7168, 4, 2, S)
        TMP = [ar(512 * j, 512) for j in range(4)]
        CSB = [ar(2048 + 512 * z, 2, S) for z in range(2)]
        CZ = [ar(3072 + 520 * z, 2, S + 4) for z in range(2)]
        CV = [ar(4112 + 512 * z, 2, S) for z in range(2)]

        PEB = [PB[:, b, :] for b in range(4)]

        @block.tensor
        def _(pe):
            n = Count()

            def claim(b, counted=True):
                if n.uses[b]:
                    pe.wait_ge(p_free[b], n.uses[b])
                n.uses[b] += counted

            def read(b):
                pe.wait_ge(p_free[b], n.uses[b])

            def yclaim(t, counted=False):
                if n.yuses[t]:
                    pe.wait_ge(y_free[t], n.yuses[t])
                n.yuses[t] += counted

            def unit(i=0):
                pe.wait_ge(s["w_split"], n.v + 1 + i * RING)
                n.v += 1
                return (n.v - 1) % RING

            def split_product(out_ap, ah, al, bh, bl, start, stop):
                pe.matmul(out_ap, ah, bh, start=start, stop=False)
                pe.matmul(out_ap, ah, bl, start=False, stop=False)
                return pe.matmul(out_ap, al, bh, start=False, stop=stop)

            def cols_T(bank, i=0, xh=XTH, xl=XTL):
                slot = unit(i)
                for j in range(2):
                    for k in range(KC):
                        w = slice(k * UC + j * P, k * UC + j * P + P)
                        mm = split_product(PB[:, bank, j * S:(j + 1) * S], HI[:, slot, w], LO[:, slot, w],
                                           xh[:, k, :], xl[:, k, :], k == 0, k == KC - 1)
                mm.then_inc(s["w_used"], 1)

            def cols_N(bank, kc=KC, cols=UC, xh=XTH, xl=XTL, k0=0):
                slot = unit()
                for t in range(NT):
                    for k in range(kc):
                        w = slice(k * cols, (k + 1) * cols)
                        x = slice(t * P, (t + 1) * P)
                        mm = split_product(PB[:, bank, t * UC:t * UC + cols], xh[:, k0 + k, x], xl[:, k0 + k, x],
                                           HI[:, slot, w], LO[:, slot, w], k == 0, k == kc - 1)
                mm.then_inc(s["w_used"], 1)

            def rows(ah, al, k0, start, stop, i=0):
                slot = unit(i)
                for k in range(2):
                    for t in range(NT):
                        for h in range(2):
                            w = slice(k * D + h * 512, k * D + h * 512 + 512)
                            x = slice(t * P, (t + 1) * P)
                            mm = split_product(Y[:, t, h * 512:(h + 1) * 512], ah[:, k0 + k, x], al[:, k0 + k, x],
                                               HI[:, slot, w], LO[:, slot, w], start and k == 0, stop and k == 1)
                mm.then_inc(s["w_used"], 1)

            def out_rows():
                yclaim(0)
                yclaim(1)
                pe.wait_ge(s["ct_lo"], n.next("ct", 4))
                for r in range(4):
                    rows(CTH, CTL, 2 * r, r == 0, r == 3)

            def transposes(ready, count):
                pe.wait_ge(s[ready], count)
                for b in range(4):
                    claim(b)
                    for c in range(2):
                        for t in range(NT):
                            mm = pe.transpose(PB[:, b, c * S + t * P:c * S + (t + 1) * P],
                                              XN[:, t, (2 * b + c) * P:(2 * b + c + 1) * P], IDENT[:, :])
                    mm.then_inc(s["tp_full"], 1)

            def xt_ready():
                for b in range(4):
                    read(b)

            def attention(q, k, v, PN, PT, ylast, causal):
                for h in range(4):
                    claim(h)
                    for t in range(NT):
                        ns = P if causal and t == 0 else S
                        mm = pe.matmul(PB[:, h, t * S:t * S + ns], q(h, t), k(h, ns), start=True, stop=True)
                    mm.then_inc(s["sc_full"], 1)
                for h in range(4):
                    claim(h)
                    for j in range(2):
                        for t in range(j if causal else 0, NT):
                            mm = pe.transpose(PB[:, h, j * S + t * P:j * S + (t + 1) * P],
                                              PN[:, h, t, j * P:(j + 1) * P], IDENT[:, :])
                    mm.then_inc(s["at_full"], 1)
                for h in range(4):
                    read(h)
                    o = ylast(h)
                    t0 = 0
                    if causal:
                        t0 = P
                        pe.matmul(o[:, 0:P], v(h, 0), PT[:, h, 0, 0:P], start=True, stop=True)
                    pe.matmul(o[:, t0:S], v(h, 0), PT[:, h, 0, t0:S], start=True, stop=False)
                    mm = pe.matmul(o[:, t0:S], v(h, 1), PT[:, h, 1, t0:S], start=False, stop=True)
                mm.then_inc(s["ao_full"], 1)

            def mem_attention(layer, QM, PN, PT):
                def r(h):
                    return slice(64 * (h % 2), 64 * (h % 2) + 64)
                yclaim(0)
                attention(lambda h, t: QM[r(h), h // 2, t * P:(t + 1) * P],
                          lambda h, ns: MK[r(h), layer, h // 2, 0:ns],
                          lambda h, j: MV[:, layer, j, h * 64:(h + 1) * 64], PN, PT,
                          lambda h: Y[r(h), 0, (h // 2) * S:(h // 2 + 1) * S], False)

            def ffn(chunks, peel):
                def gate_up(i=0, uses=None, first=False):
                    if uses is None:
                        claim(0)
                    else:
                        pe.wait_ge(p_free[0], uses + i)
                    cols_T(0, i)
                    if first:
                        read(1)
                    else:
                        pe.wait_ge(s["h_mul"], n.next("hm") + i)
                    cols_T(1, i)

                def down(i, start, stop):
                    pe.wait_ge(s["h_lo"], n.next("h") + i)
                    rows(HH, HL, 0, start, stop, i)

                loops = chunks - 2 - peel
                gate_up(first=True)
                yield
                gate_up()
                yclaim(0)
                yclaim(1)
                down(0, True, False)
                v0, uses = n.v, n.uses[0]
                with pe.Fori(0, loops) as i:
                    gate_up(i, uses)
                    down(i, False, False)
                n.v = v0 + RING * loops
                n.n["h"] += loops - 1
                n.n["hm"] += loops - 1
                n.uses[0] += loops
                for j in range(1 + loops, chunks - 1):
                    gate_up()
                    down(0, False, False)
                n.next("hm")
                down(0, False, True)

            def moe(layer):
                xt_ready()
                pe.wait_ge(s["rw_ready"], 1)
                claim(2, counted=False)
                for t in range(NT):
                    for k in range(KC):
                        x = slice(t * P, (t + 1) * P)
                        mm = split_product(PB[:, 2, t * 32:t * 32 + 20], XTH[:, k, x], XTL[:, k, x],
                                           RWH[:, layer, k, :], RWL[:, layer, k, :], k == 0, k == KC - 1)
                mm.then_inc(s["rt_full"], 1)
                f = ffn(EXPERTS, 0)
                next(f)
                pe.wait_ge(s["gt_ready"], layer + 1)
                claim(3, counted=False)
                for t in range(NT):
                    mm = pe.transpose(PB[0:EXPERTS, 3, t * P:(t + 1) * P], SM[:, 64 + t * 16:80 + t * 16], IDENT[:, :])
                mm.then_inc(s["rt_full"], 1)
                for _ in f:
                    pass

            def swiglu(peel=0):
                xt_ready()
                for _ in ffn(D_FF // UC, peel):
                    pass

            pe.wait_ge(s["pool_const"], 1)
            pe.wait_ge(s["par_in"], 16 * 12)
            for b, rows_ in ((2, 70), (3, 85)):
                claim(b)
                pe.transpose(PB[:, b, 0:rows_], SM[0:rows_, (b - 2) * P:(b - 1) * P], IDENT[0:rows_, 0:rows_])\
                    .then_inc(s["tp_full"], 1)
            transposes("mem_in", 16 * NT)
            xt_ready()
            cols_T_mem = dict(xh=CTH, xl=CTL)
            claim(0)
            cols_T(0, **cols_T_mem)
            claim(1)
            cols_N(1, **cols_T_mem)
            pe.wait_ge(s["x_in"], 16)
            for b in range(4):
                claim(b)
                for c in range(2):
                    for t in range(NT):
                        mm = pe.transpose(PB[:, b, c * S + t * P:c * S + (t + 1) * P],
                                          X[:, t, (2 * b + c) * P:(2 * b + c + 1) * P], IDENT[:, :])
                mm.then_inc(s["tp_full"], 1)
            xt_ready()
            for j in range(9):
                if 4 <= j < 7:
                    pe.wait_ge(s["lf_done"], j - 3)
                claim(j % 4, counted=j >= 3)
                (cols_T if j < 6 else cols_N)(j % 4)

            def level(m, blocks):
                yclaim(m % 2, True)
                for o, lhs, rhs in blocks:
                    mm = pe.matmul(Y[:, m % 2, o:o + rhs.free_size()], lhs, rhs, start=True, stop=True)
                mm.then_inc(s["lvl_full"], 1)

            def blk(v, b):
                return v[:, b * P:(b + 1) * P]

            side = [("T", 1), ("T", 2), ("T", 3), ("T", 0), ("Tm", 1), ("Nm", 2)]
            pe.wait_ge(s["q_ready"], 1)
            for m in range(2):
                level(m, [(j * P, blk(KK, 6 * m + j), blk(Q, 6 * m + j)) for j in range(6)])
            for m, B in enumerate(LEVELS + [2 * P], 2):
                if m - 2 < len(side):
                    kind, b = side[m - 2]
                    claim(b)
                    (cols_N if kind[0] == "N" else cols_T)(b, **(cols_T_mem if kind[1:] else {}))
                pe.wait_ge(s["m_low"], m - 1)
                pe.wait_ge(s["m_high"], m - 1)
                M = MB[m % 2]
                if B <= P:
                    half = B // 2
                    level(m, [(j * 64, blk(M, j),
                               blk(M, j).rearrange("p (n b) -> p n b", b=B)[:, :, half:B]) for j in range(12)])
                else:
                    level(m, [(j * P, blk(M, 2 * j), blk(M, 2 * j + 1)) for j in range(6)])
            yclaim(0, True)
            yclaim(1, True)
            for h in range(HEADS_A):
                o = Y[:, h // 4, (h % 4) * S:(h % 4 + 1) * S]
                c = slice(h * P, (h + 1) * P)
                pe.matmul(o[:, 0:P], V0[:, 0, c], ATD[:, 2 * h, :], start=True, stop=True)
                pe.matmul(o[:, P:S], V0[:, 0, c], ATX[:, h, :], start=True, stop=False)
                mm = pe.matmul(o[:, P:S], V0[:, 1, c], ATD[:, 2 * h + 1, :], start=False, stop=True)
                if h % 2:
                    mm.then_inc(s["o_full"], 1)
            for j in range(3):
                claim(j, counted=False)
                pe.wait_ge(s["sq_done"], j + 1)
                pe.matmul(PB[:, j, :], ONES[:, :], MB[0][:, j * 512:(j + 1) * 512], start=True, stop=True)\
                    .then_inc(s["ss_full"], 1)
            pe.wait_ge(s["rt_done"], 3)
            mem_attention(0, QM0, PN0, PT0)
            out_rows()
            transposes("xn_ready", 2)
            moe(0)
            transposes("xn_ready", 4)
            xt_ready()
            for j in range(10):
                claim(j % 4)
                (cols_N if 3 <= j < 6 else cols_T)(j % 4)

            def z_product(h, out_ap, stop):
                r, c = slice(64 * (h % 2), 64 * (h % 2) + 64), h // 2
                pe.matmul(out_ap[:, 0:S], KB[r, c, 0:P], QB[r, c, :], start=True, stop=stop)
                return pe.matmul(out_ap[:, S:S + P], KB[r, c, P:S], QB[r, c, P:S], start=stop, stop=stop)

            def z_head(h):
                claim(h % 2, counted=False)
                if h >= 2:
                    pe.wait_ge(s["sp_ready"], h - 1)
                z_product(h, PB[:, h % 2, :], True).then_inc(s["z_full"], 1)

            for b in range(4):
                read(b)
            yclaim(0)
            yclaim(1)
            z_head(0)
            for h in range(HEADS_B):
                if h + 1 < HEADS_B:
                    z_head(h + 1)
                b = 2 + h % 2
                claim(b, counted=False)
                la = PB[:, b, :]
                z_product(h, la, False)
                pe.wait_ge(s["sp_ready"], h + 1)
                SP = SBW[h % 2][1]
                g = dict(start=False)
                pe.matmul(la[:, P:S], NONE[:, :], SP[:, S:S + P], stop=False, **g)
                pe.matmul(la[:, 0:384], NSUF[:, :], SP[:, 0:384], stop=True, **g).then_inc(s["la_full"], 1)
                for hh in ([h - 1] if h else []) + ([h] if h == HEADS_B - 1 else []):
                    pe.wait_ge(s["am_ready"], hh + 1)
                    r, c = slice(64 * (hh % 2), 64 * (hh % 2) + 64), hh // 2
                    o = Y[r, c // 4, (c % 4) * S:(c % 4 + 1) * S]
                    AM = SBW[hh % 2][3]
                    w = slice(hh * 64, (hh + 1) * 64)
                    pe.matmul(o[:, 0:P], VB[:, 0, w], AM[:, 0:P], start=True, stop=True)
                    pe.matmul(o[:, P:S], VB[:, 0, w], AM[:, P:S], start=True, stop=False)
                    mm = pe.matmul(o[:, P:S], VB[:, 1, w], AM[:, S:S + P], start=False, stop=True)
                    mm.then_inc(s["so_full"], 1)
            pe.wait_ge(s["am_ready"], HEADS_B)
            pe.wait_ge(s["ct_lo"], n.at("ct") + 3)
            mem_attention(1, QM1, PN1, PT1)
            out_rows()
            transposes("xn_ready", 6)
            moe(1)
            transposes("xn_ready", 10)
            swiglu()
            transposes("xn_ready", 12)
            xt_ready()
            for j in range(7):
                claim(j % 4)
                cols_N(j % 4, cols=160 if j == 2 else UC)
            pe.wait_ge(s["sgw_in"], 16)
            for j in range(2):
                b = (3, 0)[j]
                claim(b)
                for g in range(4):
                    mm = pe.transpose(PB[:, b, g * P:(g + 1) * P], SGW[:, 4 * j + g, :], IDENT[:, :])
                mm.then_inc(s["sgw_tp"], 1)
            pe.wait_ge(s["cq_done"], 2 * NT)
            for b, chunks in ((1, (0, 1)), (2, (2, 3)), (3, (4,))):
                claim(b)
                for c in chunks:
                    for t in range(NT):
                        mm = pe.transpose(PB[:, b, (c % 2) * S + t * P:(c % 2) * S + (t + 1) * P],
                                          PRJ[:, t, c * P:(c + 1) * P], IDENT[:, :])
                mm.then_inc(s["tp_full"], 1)
            for b in (1, 2, 3):
                read(b)
            for j in range(3):
                claim(j)
                cols_N(j, kc=3, xh=CTH, xl=CTL)
            for j in range(4):
                b = (3 + j) % 4
                claim(b)
                cols_N(b, kc=2, xh=CTH, xl=CTL, k0=3)
            for b in range(4):
                read(b)
            pe.wait_ge(s["q_ev"], 2)
            for j in range(8):
                b = (3 + j) % 4
                claim(b)
                src = QN if j < 4 else KF
                for h in range(2):
                    for t in range(NT):
                        c = slice((2 * (j % 4) + h) * QKH, (2 * (j % 4) + h + 1) * QKH)
                        mm = pe.transpose(PB[0:QKH, b, h * S + t * P:h * S + (t + 1) * P], src[:, t, c], IDENT[:, :])
                mm.then_inc(s["qt_full"], 1)
            pe.wait_ge(s["vn_ready"], NT)
            yclaim(1)
            for g in range(8):
                mm = pe.matmul(Y[:, 1, g * P:(g + 1) * P], SGWT[:, g, :], ZG[:, :, 512 + g * 64:512 + (g + 1) * 64],
                               start=True, stop=True)
            mm.then_inc(s["mix_full"], 1)
            for b in range(4):
                read(b)
            yclaim(0)
            for q4 in range(2):
                def hd(h, q4=q4):
                    return 4 * q4 + h
                attention(lambda h, t: QT[0:QKH, hd(h), t * P:(t + 1) * P],
                          lambda h, ns: KT[0:QKH, hd(h), 0:ns],
                          lambda h, j: VV[:, j, hd(h) * 64:(hd(h) + 1) * 64], PN2, PT2,
                          lambda h: Y[64 * (h % 2):64 * (h % 2) + 64, 0, (hd(h) // 2) * S:(hd(h) // 2 + 1) * S], True)
            pe.wait_ge(s["sgo_ready"], 1)
            for b in range(2):
                claim(b, counted=False)
                for c in range(2):
                    for t in range(NT):
                        mm = pe.transpose(PB[:, b, c * S + t * P:c * S + (t + 1) * P],
                                          ZG[:, t, (2 * b + c) * P:(2 * b + c + 1) * P], IDENT[:, :])
                mm.then_inc(s["tp_full"], 1)
            out_rows()
            transposes("xn_ready", 14)
            swiglu()
            transposes("xn_ready", 16)
            swiglu()
            transposes("xn_ready", 18)
            xt_ready()
            for j in range(12):
                if j >= 4 and (j - 4) % 3 == 2:
                    pe.wait_ge(s["conv_done"], (j - 4) // 3 + 1)
                claim(j % 4, counted=j % 3 != 2)
                cols_T(j % 4)
            out_rows()
            transposes("xn_ready", 20)
            swiglu(peel=1)
            assert n.v == STREAM_UNITS, n.v

        @block.scalar
        def _(act):
            n = Count()

            def did(ins, name="act_chain"):
                ins.then_inc(s[name], 1)
                return n.next(name)

            def after(ins, name="act_chain"):
                act.wait_ge(s[name], did(ins, name))

            def split(k=1, i=0):
                for _ in range(k):
                    if n.u >= STREAM_UNITS:
                        return
                    slot = n.u % RING
                    act.wait_ge(raw_in[slot], 16 * (n.u // RING + 1) + 16 * i)
                    if n.u >= RING:
                        act.wait_ge(s["w_used"], n.u - RING + 1 + i * RING)
                    w = UNIT if not isinstance(i, int) else unit_width(n.u)
                    act.activation(HI[:, slot, 0:w], RAW[:, slot, 0:w], ACT.Copy).then_inc(s["w_hi"], 1)
                    n.u += 1

            def used(i=0):
                n.v += 1
                act.wait_ge(s["w_used"], n.v + i * RING)

            def transposed(xh, banks, free=True):
                for b, c, w in banks:
                    act.wait_ge(s["tp_full"], n.next("tp"))
                    act.activation(xh[:, c:c + w // S, :], PB[:, b, 0:w], ACT.Copy).then_inc(s["tp_hi"], 1)

            def scaled(g, b_, xh, banks=((0, 0, 2), (1, 2, 2), (2, 4, 2), (3, 6, 2))):
                for j, (b, c, k) in enumerate(banks):
                    act.wait_ge(s["tp_full"], n.next("tp"))
                    tmp = TMP[j]
                    used_ = n.next("tmp")
                    act.wait_ge(s["tmp_d"], used_)
                    if k == 2:
                        bias = PV[:, b_ + c + 1:b_ + c + 2] if b_ is not None else COLS[:, 1:2]
                        after(act.activation(tmp[:, S:2 * S], PB[:, b, S:2 * S], ACT.Identity,
                                             bias=bias, scale=PV[:, g + c + 1:g + c + 2]))
                    act.activation(xh[:, c:c + k, :], tmp[:, 0:k * S], ACT.Copy).then_inc(s["tp_hi"], 1)

            def root(k):
                act.wait_ge(s["n_dve"], n.next("nd"))
                act.activation(ST[:, 0:k, 14:15], ST[:, 0:k, 13:14], ACT.Sqrt).then_inc(s["n_act"], 1)

            def squares(width, src, dst):
                for t in range(NT):
                    act.wait_ge(s["x_sum"], n.next("sq"))
                    act.activation(dst(t), src(t), ACT.Square, accum_out=ST[:, t, 12:13]).then_inc(s["sq_sum"], 1)
                root(NT)

            def rms():
                squares(D, lambda t: X[:, t, :], lambda t: XN[:, t, :])

            def attention(PN, PT, causal):
                for h in range(4):
                    act.wait_ge(s["mx_ready"], n.next("mx"))
                    for t in range(NT):
                        ns = P if causal and t == 0 else S
                        act.activation(PN[:, h, t, 0:ns], PB[:, h, t * S:t * S + ns], ACT.Exp,
                                       bias=SM[:, 272 + 2 * h + t:273 + 2 * h + t],
                                       accum_out=SM[:, 280 + 2 * h + t:281 + 2 * h + t]).then_inc(s["pe_done"], 1)
                for h in range(4):
                    act.wait_ge(s["at_full"], n.next("at"))
                    if causal:
                        after(act.activation(PT[:, h, 0, :], PB[:, h, 0:S], ACT.Copy))
                        act.activation(PT[:, h, 1, P:S], PB[:, h, S + P:2 * S], ACT.Copy).then_inc(p_free[h], 1)
                    else:
                        act.activation(PT[:, h, :, :], PB[:, h, :], ACT.Copy).then_inc(p_free[h], 1)

            def mixed(c, src):
                act.activation(CTH[:, c:c + 2, :], src, ACT.Copy).then_inc(s["ct_hi"], 1)

            def ffn(chunks, peel, gated):
                def gate(i=0):
                    used(i)
                    act.activation(SG[:, :], PB[:, 0, :], ACT.Silu).then_inc(p_free[0], 1)
                    split(1, i)

                def up(i=0):
                    used(i)
                    split(1, i)

                def hidden(i=0, down=True):
                    if down:
                        used(i)
                    if gated:
                        act.wait_ge(s["h_gb"], n.next("hg") + i)
                    act.wait_ge(s["h_mul"], n.next("hm") + i)
                    act.activation(HH[:, :, :], HT[:, :], ACT.Copy).then_inc(s["h_hi"], 1)
                    if down:
                        split(1, i)

                gate()
                up()
                act.wait_ge(s["h_mul"], n.at("hm") + 1)
                gate()
                hidden(down=False)
                up()
                hidden()
                loops = chunks - 2 - peel
                u0, v0 = n.u, n.v
                with act.Fori(0, loops) as i:
                    gate(i)
                    up(i)
                    hidden(i)
                n.u, n.v = u0 + RING * loops, v0 + RING * loops
                n.n["hm"] += loops - 1
                if gated:
                    n.n["hg"] += loops - 1
                for j in range(1 + loops, chunks - 1):
                    gate()
                    up()
                    hidden()
                used()
                split()

            def moe():
                act.wait_ge(s["r_dve"], n.next("rd"))
                act.activation(SM[:, 128:136], SM[:, 128:136], ACT.Exp).then_inc(s["r_act"], 1)
                act.wait_ge(s["r_dve"], n.next("rd"))
                act.activation(SM[:, 190:192], SM[:, 190:192], ACT.Exp).then_inc(s["r_act"], 1)
                ffn(EXPERTS, 0, True)

            r1 = [("ln_mix_g", 16), ("ln_mix_b", 16), ("ln_ffn_g", 16), ("ln_ffn_b", 16), ("a_gnorm", 6)]
            r2 = [("ffn_pre_norm_2", 16), ("mix_norm_2", 16), ("ffn_post_norm_2", 16)]
            for base, rows_ in ((0, r1), (P, r2)):
                at = 0
                for name, k in rows_:
                    act.dma_start(SM[at:at + k, base:base + P], a[name].rearrange("l (k p) -> (l k) p", p=P))\
                        .then_inc(s["par_in"], 16)
                    at += k
            act.dma_start(SM[48:72, P:2 * P], a["conv_w_2"][0].rearrange("j (k p) -> (j k) p", p=P)).then_inc(s["par_in"], 16)
            act.dma_start(SM[72:75, P:2 * P], a["q_norm_2"].rearrange("l (k p) -> (l k) p", p=P)).then_inc(s["par_in"], 16)
            act.dma_start(SM[75:77, P:2 * P], a["kv_norm_2"].rearrange("l (k p) -> (l k) p", p=P)).then_inc(s["par_in"], 16)
            act.dma_start(SM[77:85, P:2 * P], a["sg_b_2"][0]).then_inc(s["par_in"], 16)
            for layer in range(2):
                act.dma_start(RWR[:, layer, :, 0:4], a["w_group"][layer].rearrange("(k p) e -> p k e", p=P)).then_inc(s["rw_in"], 16)
                act.dma_start(RWR[:, layer, :, 4:20], a["w_router"][layer].rearrange("(k p) e -> p k e", p=P)).then_inc(s["rw_in"], 16)
                act.dma_start(RB[:, layer, 0:4], a["b_group"][layer].partition_broadcast(P)).then_inc(s["rb_in"], 16)
                act.dma_start(RB[:, layer, 4:20], a["b_router"][layer].partition_broadcast(P)).then_inc(s["rb_in"], 16)
            act.wait_ge(s["tp_full"], n.next("tp", 2))
            act.activation(PV[:, 0:70], PB[:, 2, 0:70], ACT.Copy).then_inc(p_free[2], 1)
            act.activation(PV[:, 70:155], PB[:, 3, 0:85], ACT.Copy).then_inc(p_free[3], 1)
            act.wait_ge(s["rw_in"], 16 * 4)
            act.activation(RWH[:, :, :, :], RWR[:, :, :, :], ACT.Copy).then_inc(s["rw_hi"], 1)
            full = [(b, 2 * b, 512) for b in range(4)]
            transposed(CTH, full)
            split(RING)
            used()
            act.activation(MK[:, 0, :, :], PB[:, 0, :], ACT.Copy).then_inc(p_free[0], 1)
            split()
            used()
            act.activation(MV[:, 0, :, :], PB[:, 1, :], ACT.Copy).then_inc(p_free[1], 1)
            split()
            transposed(XTH, full)
            for j in range(3):
                L = MB[0][:, j * 512:(j + 1) * 512]
                used()
                after(act.activation(L, PB[:, j, :], ACT.Abs))
                after(act.activation(L, L, ACT.Exp, scale=-1.0))
                did(act.activation(L, L, ACT.Ln, bias=COLS[:, 0:1]), "f_act")
                act.wait_ge(s["lf_done"], j + 1)
                did(act.activation(KK[:, j * 512:(j + 1) * 512], MB[1][:, j * 512:(j + 1) * 512], ACT.Exp))
                split()
            for j in range(3):
                used()
                act.activation(Q[:, j * 512:(j + 1) * 512], PB[:, (3 + j) % 4, :], ACT.Silu)\
                    .then_inc(p_free[(3 + j) % 4], 1)
                split()
            for j in range(3):
                used()
                act.activation(V0[:, :, j * S:(j + 1) * S], PB[:, (6 + j) % 4, :].rearrange("p (t c) -> p t c", t=NT),
                               ACT.Copy).then_inc(p_free[(6 + j) % 4], 1)
                split()
            for m in range(2, 10):
                if m < 8:
                    used()
                    j = m - 2
                    b = (1, 2, 3, 0, 1, 2)[j]
                    if j == 0:
                        ins = act.activation(QM0[:, :, :], PB[:, b, :], ACT.Copy, scale=0.125)
                    elif j < 4:
                        ins = act.activation(GS[:, (j - 1) * 512:j * 512], PB[:, b, :], ACT.Copy)
                    else:
                        dst = (MK, MV)[j - 4]
                        ins = act.activation(dst[:, 1, :, :], PB[:, b, :], ACT.Copy)
                    ins.then_inc(p_free[b], 1)
                    split()
                act.wait_ge(s["dlow"], m - 1)
                act.wait_ge(s["dhigh"], m - 1)
                act.activation(MB[m % 2], MB[m % 2], ACT.Exp).then_inc(s["e_done"], 1)
            act.wait_ge(s["w_hi"], n.u)
            after(act.activation(GS[:, :], GS[:, :], ACT.Silu), "gs_ready")
            for j in range(3):
                act.wait_ge(s["o_full"], j + 1)
                act.activation(MB[0][:, j * 512:(j + 1) * 512], Y[:, j // 2, (j % 2) * 512:(j % 2 + 1) * 512],
                               ACT.Square).then_inc(s["sq_done"], 1)
            for j in range(3):
                act.wait_ge(s["ss_full"], j + 1)
                act.activation(MB[1][:, j * 512:(j + 1) * 512], PB[:, j, :], ACT.Sqrt, scale=1.0 / P,
                               bias=COLS[:, 2:3]).then_inc(s["rt_done"], 1)
            for j in range(3):
                act.wait_ge(s["o_norm"], j + 1)
                mixed(2 * j, G[:, j * 512:(j + 1) * 512])
            attention(PN0, PT0, False)
            act.wait_ge(s["ao_full"], 1)
            mixed(6, Y[:, 0, 0:512])

            def mixer_out():
                for _ in range(4):
                    used()
                    split()

            mixer_out()
            root(NT)
            scaled(0, 16, XTH)
            moe()
            root(NT)
            scaled(32, 48, XTH)
            for j in range(10):
                b = j % 4
                used()
                if j < 3:
                    ins = act.activation(KB[:, 2 * j:2 * j + 2, :], PB[:, b, :], ACT.Copy)
                elif j < 6:
                    ins = act.activation(VB[:, :, (j - 3) * S:(j - 2) * S], PB[:, b, :].rearrange("p (t c) -> p t c", t=NT), ACT.Copy)
                elif j < 9:
                    ins = act.activation(QB[:, 2 * (j - 6):2 * (j - 5), :], PB[:, b, :], ACT.Copy, scale=0.125)
                else:
                    ins = act.activation(QM1[:, :, :], PB[:, b, :], ACT.Copy, scale=0.125)
                ins.then_inc(p_free[b], 1)
                split()
            def soft(h):
                A = SBW[h % 2][0]
                act.wait_ge(s["z_full"], h + 1)
                if h >= 2:
                    act.wait_ge(s["sp_ready"], h - 1)
                after(act.activation(A, PB[:, h % 2, 0:384], ACT.Abs))
                after(act.activation(A, A, ACT.Exp, scale=-1.0))
                act.activation(A, A, ACT.Ln, bias=COLS[:, 0:1]).then_inc(s["sp_act"], 1)

            soft(0)
            for h in range(HEADS_B):
                if h + 1 < HEADS_B:
                    soft(h + 1)
                act.wait_ge(s["lmin"], h + 1)
                EA, AM = SBW[h % 2][2:4]
                if h >= 2:
                    act.wait_ge(s["so_full"], h - 1)
                did(act.activation(AM[:, P:S], PB[:, 2 + h % 2, P:S], ACT.Exp))
                la = PB[:, 2 + h % 2, 0:512].rearrange("p (a b) -> p a b", b=S)[:, :, 0:P]
                ea = EA.rearrange("p (a b) -> p a b", b=P)[:, 0:2, :]
                act.activation(ea, la, ACT.Exp).then_inc(s["ea_done"], 1)
            for j in range(3):
                act.wait_ge(s["so_full"], 4 * (j + 1))
                mixed(2 * j, Y[:, j // 2, (j % 2) * 512:(j % 2 + 1) * 512])
            attention(PN1, PT1, False)
            act.wait_ge(s["ao_full"], 2)
            mixed(6, Y[:, 0, 0:512])
            mixer_out()
            root(NT)
            scaled(8, 24, XTH)
            moe()
            root(NT)
            rms()
            scaled(70, None, XTH)
            ffn(D_FF // UC, 0, False)
            rms()
            scaled(70 + 16, None, XTH)
            act.wait_ge(s["rope_cs"], 1)
            after(act.activation(SM[:, 320:384], SM[:, 320:384], ACT.Sin), "rope_act")
            for j in range(7):
                b = j % 4
                used()
                src = PB[:, b, :].rearrange("p (t c) -> p t c", t=NT)
                if j < 3:
                    w = 160 if j == 2 else UC
                    act.activation(PRJ[:, :, j * UC:j * UC + w], src[:, :, 0:w], ACT.Copy).then_inc(p_free[b], 1)
                else:
                    act.activation(ZG[:, :, (j - 3) * UC:(j - 2) * UC], src, ACT.Gelu).then_inc(p_free[b], 1)
                split()
            act.wait_ge(s["w_hi"], n.u)
            for k, (lo, hi, src) in enumerate(((0, 384, PRJ), (384, 640, PRJ), (512, 1024, ZG))):
                for t in range(NT):
                    act.activation(SG[:, 0:hi - lo], src[:, t, lo:hi], ACT.Square,
                                   accum_out=SM[:, 300 + 2 * k + t:301 + 2 * k + t]).then_inc(s["cq_act"], 1)
                    act.wait_ge(s["cq_act"], n.next("cqa"))
            act.wait_ge(s["n_dve"], n.next("nd"))
            act.activation(SM[:, 300:306], SM[:, 300:306], ACT.Sqrt).then_inc(s["n_act"], 1)
            scaled(70 + 72, None, CTH, banks=((1, 0, 2), (2, 2, 2), (3, 4, 1)))
            for j in range(3):
                used()
                act.activation(QN[:, :, j * S:(j + 1) * S], PB[:, j, :].rearrange("p (t c) -> p t c", t=NT), ACT.Copy,
                               scale=QKH ** -0.5).then_inc(p_free[j], 1)
                split()
            for j in range(4):
                b = (3 + j) % 4
                used()
                src = PB[:, b, :].rearrange("p (t h c) -> p t h c", t=NT, h=2)
                act.activation(KF.rearrange("p t (h c) -> p t h c", c=QKH)[:, :, 2 * j:2 * j + 2, 0:NOPE],
                               src[:, :, :, 0:64], ACT.Copy)
                act.activation(VV[:, :, j * P:(j + 1) * P].rearrange("p t (h c) -> p t h c", c=64),
                               src[:, :, :, 64:128], ACT.Copy).then_inc(p_free[b], 1)
                split()
            for j in range(8):
                b = (3 + j) % 4
                act.wait_ge(s["qt_full"], j + 1)
                dst = QT if j < 4 else KT
                act.activation(dst[0:QKH, 2 * (j % 4):2 * (j % 4) + 2, :], PB[0:QKH, b, :], ACT.Copy).then_inc(p_free[b], 1)
            attention(PN2, PT2, True)
            attention(PN2, PT2, True)
            for j in range(2):
                act.wait_ge(s["ao_full"], 4)
                mixed(2 * j, Y[:, 0, j * 512:(j + 1) * 512])
            for b in range(2):
                act.wait_ge(s["tp_full"], n.next("tp"))
                mixed(4 + 2 * b, PB[:, b, :])
            mixer_out()
            rms()
            scaled(70 + 32, None, XTH)
            ffn(D_FF // UC, 0, False)
            rms()
            scaled(70 + 8, None, XTH)
            ffn(D_FF // UC, 0, False)
            rms()
            scaled(70 + 24, None, XTH)
            for j in range(4):
                used()
                b = (3 * j) % 4
                if j >= 2:
                    act.wait_ge(s["conv_done"], j - 1)
                act.activation(CSB[j % 2][:, :, :], PB[:, b, :], ACT.Copy).then_inc(p_free[b], 1)
                split()
                used()
                split()
                used()
                act.wait_ge(s["conv_done"], j + 1)
                mixed(2 * j, CV[j % 2][:, :, :])
                split()
            mixer_out()
            rms()
            scaled(70 + 40, None, XTH)
            ffn(D_FF // UC, 1, False)
            squares(D, lambda t: X[:, t, :], lambda t: XN[:, t, :])
            assert n.u == n.v == STREAM_UNITS, (n.u, n.v)

        @block.vector
        def _(dve):
            n = Count()

            def did(ins, name="dve_chain"):
                ins.then_inc(s[name], 1)
                return n.next(name)

            def after(ins, name="dve_chain"):
                dve.wait_ge(s[name], did(ins, name))

            def split(k=1, i=0):
                for _ in range(k):
                    if n.u >= STREAM_UNITS:
                        return
                    slot = n.u % RING
                    dve.wait_ge(s["w_hi"], n.u + 1 + i * RING)
                    w = UNIT if not isinstance(i, int) else unit_width(n.u)
                    dve.tensor_tensor(LO[:, slot, 0:w], RAW[:, slot, 0:w], HI[:, slot, 0:w].bitcast(F32),
                                      ALU.subtract).then_inc(s["w_split"], 1)
                    n.u += 1

            def used(i=0):
                n.v += 1
                dve.wait_ge(s["w_used"], n.v + i * RING)

            def rest(lo, src, hi):
                return dve.tensor_tensor(lo, src, hi.bitcast(F32), ALU.subtract)

            def transposed(xh, xl):
                for b in range(4):
                    dve.wait_ge(s["tp_hi"], n.next("tph"))
                    rest(xl[:, 2 * b:2 * b + 2, :], PB[:, b, :], xh[:, 2 * b:2 * b + 2, :]).then_inc(p_free[b], 1)

            def scaled(g, b_, xh, xl, banks=((0, 0, 2), (1, 2, 2), (2, 4, 2), (3, 6, 2))):
                def low(j):
                    b, c, k = banks[j]
                    dve.wait_ge(s["tp_hi"], n.next("tph"))
                    rest(xl[:, c:c + k, :], TMP[j][:, 0:k * S], xh[:, c:c + k, :]).then_inc(p_free[b], 1)
                for j, (b, c, k) in enumerate(banks):
                    dve.wait_ge(s["tp_full"], n.next("tp"))
                    tmp = TMP[j][:, 0:S]
                    if b_ is None:
                        dve.tensor_scalar(tmp, PB[:, b, 0:S], PV[:, g + c:g + c + 1], None, ALU.mult)\
                            .then_inc(s["tmp_d"], 1)
                    else:
                        dve.tensor_scalar(tmp, PB[:, b, 0:S], PV[:, g + c:g + c + 1], PV[:, b_ + c:b_ + c + 1],
                                          ALU.mult, ALU.add).then_inc(s["tmp_d"], 1)
                    if j:
                        low(j - 1)
                low(len(banks) - 1)

            def rooted(scale, eps):
                col = 13 if scale is None else 12
                dve.tensor_scalar(ST[:, :, 13:14], ST[:, :, col:col + 1], scale or 1.0, eps, ALU.mult, ALU.add)\
                    .then_inc(s["n_dve"], 1)
                dve.wait_ge(s["n_act"], n.next("na"))
                after(dve.reciprocal(ST[:, :, 15:16], ST[:, :, 14:15]))

            def layer_norm(g, b_, xt=True):
                dve.wait_ge(s["x_ready"] if n.at("xr") else s["x_in"], n.at("xr") or 16)
                for t in range(NT):
                    did(dve.scalar_tensor_tensor(out=XN[:, t, :], in0=X[:, t, :], scalar=ALPHA, in1=Y[:, t, :],
                                                 op0=ALU.mult, op1=ALU.add))
                dve.wait_ge(s["dve_chain"], n.at("dve_chain"))
                for t in range(NT):
                    for h in range(2):
                        did(dve.bn_stats(ST[:, t, 6 * h:6 * h + 6], XN[:, t, h * 512:(h + 1) * 512]))
                dve.wait_ge(s["dve_chain"], n.at("dve_chain"))
                for t in range(NT):
                    did(dve.bn_aggr(ST[:, t, 12:14], ST[:, t, 0:12]))
                dve.wait_ge(s["dve_chain"], n.at("dve_chain"))
                rooted(None, LN_EPS)
                for t in range(NT):
                    dve.tensor_scalar(XN[:, t, :], XN[:, t, :], ST[:, t, 12:13], ST[:, t, 15:16], ALU.subtract, ALU.mult)\
                        .then_inc(s["xn_ready"], 1)
                n.next("xr", 2)
                split()
                if xt:
                    scaled(g, b_, XTH, XTL)

            def residual(scale):
                for t in range(NT):
                    dve.scalar_tensor_tensor(out=X[:, t, :], in0=Y[:, t, :], scalar=scale, in1=X[:, t, :],
                                             op0=ALU.mult, op1=ALU.add).then_inc(s["x_sum"], 1)

            def rms(g, ahead=True):
                dve.wait_ge(s["sq_sum"], n.next("sqs", NT))
                rooted(1.0 / D, RMS_EPS)
                for t in range(NT):
                    dve.tensor_scalar(XN[:, t, :], X[:, t, :], ST[:, t, 15:16], None, ALU.mult)\
                        .then_inc(s["xn_ready"], 1)
                if ahead:
                    split()
                scaled(g, None, XTH, XTL)

            def mixed(c, src):
                dve.wait_ge(s["ct_hi"], n.next("cth"))
                rest(CTL[:, c:c + 2, :], src, CTH[:, c:c + 2, :]).then_inc(s["ct_lo"], 1)

            def bc(v, *shape):
                return v.broadcast_to([P, *shape])

            def attention(PN, causal):
                for h in range(4):
                    dve.wait_ge(s["sc_full"], n.next("sc"))
                    if causal:
                        diag = PB[:, h, :].rearrange("p (a b) -> p a b", b=P)[:, 0:4:3, :]
                        after(dve.tensor_tensor(diag, diag, bc(CAUS[:, :].unsqueeze(1), 2, P), ALU.add))
                        did(dve.reduce_max(SM[:, 256 + 2 * h:257 + 2 * h], PB[:, h, 0:P], axis=AX))
                        after(dve.reduce_max(SM[:, 257 + 2 * h:258 + 2 * h], PB[:, h, S:2 * S], axis=AX))
                    else:
                        after(dve.reduce_max(SM[:, 256 + 2 * h:258 + 2 * h],
                                             PB[:, h, :].rearrange("p (t m) -> p t m", t=NT), axis=AX))
                    dve.tensor_scalar(SM[:, 272 + 2 * h:274 + 2 * h], SM[:, 256 + 2 * h:258 + 2 * h], -1.0, None,
                                      ALU.mult).then_inc(s["mx_ready"], 1)
                for h in range(4):
                    dve.wait_ge(s["pe_done"], n.next("ped", 2))
                    after(dve.reciprocal(SM[:, 288 + 2 * h:290 + 2 * h], SM[:, 280 + 2 * h:282 + 2 * h]))
                    for t in range(NT):
                        ns = P if causal and t == 0 else S
                        ins = dve.tensor_scalar(PN[:, h, t, 0:ns], PN[:, h, t, 0:ns],
                                                SM[:, 288 + 2 * h + t:289 + 2 * h + t], None, ALU.mult)
                        ins.then_inc(*((p_free[h], 1) if t else (s["dve_chain"], 1)))
                    n.next("dve_chain")

            def mixer_out():
                for r in range(4):
                    used()
                    if r < 3:
                        split()

            def ffn(chunks, peel, gated):
                def mul(i=0):
                    if n.at("hh"):
                        dve.wait_ge(s["h_lo"], n.at("hh") + i)
                    dve.tensor_tensor(HT[:, :], SG[:, :], PB[:, 1, :], ALU.mult).then_inc(s["h_mul"], 1)
                    dve.wait_ge(s["h_mul"], n.next("hm") + i)

                def weigh(e):
                    if gated:
                        g = GB[:, e, :] if isinstance(e, int) else \
                            GB[:, bass.ds(e, 1), :].rearrange("p e t -> p (e t)")
                        ht = HT[:, :].rearrange("p (j t) -> p j t", j=2)
                        dve.tensor_tensor(ht, ht, bc(g.unsqueeze(1), 2, S), ALU.mult).then_inc(s["h_gb"], 1)

                def up(i=0, e=None):
                    used(i)
                    mul(i)
                    weigh(e)
                    split(1, i)

                def gate(i=0):
                    used(i)
                    split(1, i)

                def hidden(i=0, down=True):
                    if down:
                        used(i)
                    dve.wait_ge(s["h_hi"], n.next("hh") + i)
                    rest(HL[:, :, :], HT[:, :], HH[:, :, :]).then_inc(s["h_lo"], 1)
                    if down:
                        split(1, i)

                gate()
                used()
                mul()
                if gated:
                    router_gates()
                split()
                gate()
                if gated:
                    dve.wait_ge(s["gb_in"], 16 * layer_of[0])
                weigh(0)
                hidden(down=False)
                up(0, 1)
                hidden()
                loops = chunks - 2 - peel
                u0, v0 = n.u, n.v
                with dve.Fori(0, loops) as i:
                    gate(i)
                    up(i, i + 2)
                    hidden(i)
                n.u, n.v = u0 + RING * loops, v0 + RING * loops
                n.n["hh"] += loops - 1
                n.n["hm"] += loops - 1
                for j in range(1 + loops, chunks - 1):
                    gate()
                    up(0, j + 1)
                    hidden()
                used()

            def first_of(v, mx, tmp, best, pick):
                after(dve.tensor_tensor(tmp, v, bc(mx, NT, 4), ALU.is_equal))
                after(dve.tensor_tensor(tmp, tmp, bc(W4[:, :].unsqueeze(1), NT, 4), ALU.mult))
                after(dve.reduce_max(best, tmp, axis=AX))
                after(dve.tensor_tensor(pick, tmp, bc(best.unsqueeze(2), NT, 4), ALU.is_equal))

            def sm(off, *shape):
                v = SM[:, off:off + int(np.prod(shape))]
                return v if len(shape) == 1 else v.rearrange("p (a b) -> p a b", b=shape[-1])

            def router(layer):
                dve.wait_ge(s["rt_full"], 2 * layer + 1)
                lg = sm(0, NT, 20)
                after(dve.tensor_tensor(lg, PB[:, 2, 0:64].rearrange("p (t e) -> p t e", e=32)[:, :, 0:20],
                                        bc(RB[:, layer, :].unsqueeze(1), NT, 20), ALU.add))
                gl = lg[:, :, 0:4]
                gmax, gsum, ge, oh = sm(136, 2), sm(138, 2), sm(128, NT, 4), sm(148, NT, 4)
                after(dve.reduce_max(gmax, gl, axis=AX))
                dve.tensor_tensor(ge, gl, bc(gmax.unsqueeze(2), NT, 4), ALU.subtract).then_inc(s["r_dve"], 1)
                first_of(gl, gmax.unsqueeze(2), sm(140, NT, 4), sm(232, 2), oh)
                el = lg[:, :, 4:20]
                prod = sm(156, NT, 16)
                for t in range(NT):
                    did(dve.tensor_tensor(prod[:, t, :].rearrange("p (g j) -> p g j", j=4),
                                          el[:, t, :].rearrange("p (g j) -> p g j", j=4),
                                          bc(oh[:, t, :].unsqueeze(2), 4, 4), ALU.mult))
                dve.wait_ge(s["dve_chain"], n.at("dve_chain"))
                il = sm(192, NT, 4)
                for t in range(NT):
                    did(dve.reduce_sum(il[:, t, :], prod[:, t, :].rearrange("p (g j) -> p j g", j=4), axis=AX))
                dve.wait_ge(s["dve_chain"], n.at("dve_chain"))
                m1, m2, f1, f2, il2 = sm(224, 2), sm(226, 2), sm(200, NT, 4), sm(216, NT, 4), sm(208, NT, 4)
                after(dve.reduce_max(m1, il, axis=AX))
                first_of(il, m1.unsqueeze(2), sm(140, NT, 4), sm(232, 2), f1)
                after(dve.scalar_tensor_tensor(out=il2, in0=f1, scalar=NEG, in1=il, op0=ALU.mult, op1=ALU.add))
                after(dve.reduce_max(m2, il2, axis=AX))
                dve.tensor_tensor(sm(190, 2), m2, m1, ALU.subtract).then_inc(s["r_dve"], 1)
                first_of(il2, m2.unsqueeze(2), sm(140, NT, 4), sm(232, 2), f2)
                dve.wait_ge(s["r_act"], 2 * layer + 2)
                w1, w2, e = sm(228, 2), sm(230, 2), sm(190, 2)
                after(dve.reduce_sum(gsum, ge, axis=AX))
                after(dve.tensor_scalar(w1, e, 1.0, None, ALU.add))
                after(dve.tensor_tensor(w1, w1, gsum, ALU.mult))
                after(dve.reciprocal(w1, w1))
                after(dve.tensor_tensor(w2, w1, e, ALU.mult))
                after(dve.tensor_tensor(f1, f1, bc(w1.unsqueeze(2), NT, 4), ALU.mult))
                after(dve.tensor_tensor(f2, f2, bc(w2.unsqueeze(2), NT, 4), ALU.mult))
                after(dve.tensor_tensor(f1, f1, f2, ALU.add))
                for t in range(NT):
                    ins = dve.tensor_tensor(SM[:, 64 + 16 * t:80 + 16 * t].rearrange("p (g j) -> p g j", j=4),
                                            bc(oh[:, t, :].unsqueeze(2), 4, 4), bc(f1[:, t, :].unsqueeze(1), 4, 4), ALU.mult)
                    if t:
                        ins.then_inc(s["gt_ready"], 1)
                    else:
                        did(ins)

            layer_of = [0]

            def router_gates():
                dve.wait_ge(s["rt_full"], 2 * layer_of[0] + 2)
                dve.tensor_copy(SM[0:EXPERTS, 384:640], PB[0:EXPERTS, 3, 0:S]).then_inc(s["gt_sb"], 1)
                layer_of[0] += 1

            def moe(layer):
                router(layer)
                ffn(EXPERTS, 0, True)

            dve.wait_ge(s["rw_hi"], 1)
            rest(RWL[:, :, :, :], RWR[:, :, :, :], RWH[:, :, :, :]).then_inc(s["rw_ready"], 1)
            dve.wait_ge(s["rb_in"], 16 * 4)
            dve.wait_ge(s["pool_const"], 1)
            n.next("tp", 2)
            transposed(CTH, CTL)
            n.next("tp", 4)
            split(RING)
            for _ in range(2):
                used()
                split()
            transposed(XTH, XTL)
            n.next("tp", 4)
            for j in range(3):
                used()
                w = slice(j * 512, (j + 1) * 512)
                dve.wait_ge(s["f_act"], j + 1)
                after(dve.scalar_tensor_tensor(out=G[:, w], in0=PB[:, j, :], scalar=0.0, in1=MB[0][:, w],
                                               op0=ALU.min, op1=ALU.subtract))
                dve.tensor_tensor(MB[1][:, w], G[:, w], PB[:, j, :], ALU.subtract).then_inc(s["lf_done"], 1)
                dve.wait_ge(s["lf_done"], j + 1)
                for b in range(4 * j, 4 * j + 4):
                    gb = G[:, b * P:(b + 1) * P]
                    did(dve.tensor_tensor_scan(gb, ONES[:, :], gb, 0.0, ALU.mult, ALU.add), "g_ready")
                split()
            dve.wait_ge(s["g_ready"], 12)
            for j in range(3):
                used()
                split()
            did(dve.tensor_scalar(Q, Q, P ** -0.5, None, ALU.mult), "q_ready")
            for j in range(3):
                used()
                split()

            def halves(v, B):
                x = v.rearrange("p (n b) -> p n b", b=B)
                return x[:, :, 0:B // 2], x[:, :, B // 2:B]

            def decay_up(m):
                if m >= 4:
                    dve.wait_ge(s["lvl_full"], m - 1)
                if m < 9:
                    B = LEVELS[m - 2]
                    ref = halves(G, B)[0][:, :, B // 2 - 1:B // 2]
                    ins = dve.tensor_tensor(halves(MB[m % 2], B)[1], halves(G, B)[1],
                                            ref.broadcast_to([P, 1536 // B, B // 2]), ALU.subtract)
                else:
                    ins = dve.tensor_copy(halves(MB[m % 2], S)[1], halves(G, S)[1])
                ins.then_inc(s["dhigh"], 1)

            def take_level(m):
                dve.wait_ge(s["lvl_full"], m + 1)
                if m:
                    dve.wait_ge(y_free[(m - 1) % 2], (m + 1) // 2)
                y = Y[:, m % 2, 0:MIX]
                if m < 2:
                    ins = dve.copy_predicated(ATD[:, 6 * m:6 * m + 6, :],
                                              bc(MSK[:, 7, :].unsqueeze(1), 6, P), y.rearrange("p (n b) -> p n b", b=P))
                elif m < 9:
                    B = LEVELS[m - 2]
                    out_ = ATD.rearrange("p n (m b) -> p n m b", b=B)[:, :, :, B // 2:B]
                    mask = MSK[:, m - 2, :].rearrange("p (m b) -> p m b", b=B)[:, :, B // 2:B]
                    ins = dve.copy_predicated(out_, mask.unsqueeze(1).broadcast_to([P, 12, P // B, B // 2]),
                                              y.rearrange("p (n m b) -> p n m b", n=12, b=B // 2))
                else:
                    ins = dve.tensor_copy(ATX[:, :, :], y.rearrange("p (n b) -> p n b", b=P))
                ins.then_inc(y_free[m % 2], 1)

            decay_up(2)
            dve.wait_ge(s["at_ready"], 1)
            take_level(0)
            take_level(1)
            for m in range(2, 10):
                if m < 8:
                    used()
                    split()
                if m < 9:
                    decay_up(m + 1)
                dve.wait_ge(s["e_done"], m - 1)
                B = LEVELS[m - 2] if m < 9 else S
                up = halves(MB[m % 2], B)[1]
                dve.tensor_tensor(up, up, halves(Q, B)[1], ALU.mult).then_inc(s["m_high"], 1)
                if m > 2:
                    take_level(m - 1)
            take_level(9)
            for j in range(3):
                dve.wait_ge(s["rt_done"], j + 1)
                rt = MB[1][:, j * 512:(j + 1) * 512]
                t_ = G[:, j * 512:(j + 1) * 512]
                after(dve.reciprocal(rt, rt))
                ins = dve.tensor_tensor(t_, Y[:, j // 2, (j % 2) * 512:(j % 2 + 1) * 512], rt, ALU.mult)
                if j:
                    ins.then_inc(y_free[j - 1], 1)
                    dve.wait_ge(y_free[j - 1], 6)
                else:
                    after(ins)
                dve.wait_ge(s["gs_ready"], 1)
                for h in range(2):
                    w = slice(h * S, (h + 1) * S)
                    gs = GS[:, j * 512:(j + 1) * 512]
                    ins = dve.scalar_tensor_tensor(out=t_[:, w], in0=t_[:, w], scalar=PV[:, 64 + 2 * j + h:65 + 2 * j + h],
                                                   in1=gs[:, w], op0=ALU.mult, op1=ALU.mult)
                    if h:
                        ins.then_inc(s["o_norm"], 1)
                    else:
                        did(ins)
            for j in range(3):
                mixed(2 * j, G[:, j * 512:(j + 1) * 512])
            attention(PN0, False)
            mixed(6, Y[:, 0, 0:512])
            mixer_out()
            layer_norm(0, 16)
            moe(0)
            layer_norm(32, 48)
            for j in range(10):
                used()
                split()
            dve.wait_ge(s["am_zero"], 1)

            def soft(h):
                A, SP = SBW[h % 2][0:2]
                dve.wait_ge(s["sp_act"], h + 1)
                after(dve.scalar_tensor_tensor(out=SP, in0=PB[:, h % 2, 0:384], scalar=0.0, in1=A, op0=ALU.max, op1=ALU.add))
                d = SP.rearrange("p (a b) -> p a b", b=P)[:, 0:3:2, :]
                dve.tensor_tensor(d, d, bc(STRICT[:, :].unsqueeze(1), 2, P), ALU.mult).then_inc(s["sp_ready"], 1)

            soft(0)
            for h in range(HEADS_B):
                if h + 1 < HEADS_B:
                    soft(h + 1)
                dve.wait_ge(s["la_full"], h + 1)
                la = PB[:, 2 + h % 2, 0:384]
                dve.tensor_scalar(la, la, 0.0, None, ALU.min).then_inc(s["lmin"], 1)
                dve.wait_ge(s["ea_done"], h + 1)
                EA, AM = SBW[h % 2][2:4]
                dve.copy_predicated(AM.rearrange("p (a b) -> p a b", b=P)[:, 0:3:2, :],
                                    bc(MSK[:, 8, :].unsqueeze(1), 2, P),
                                    EA.rearrange("p (a b) -> p a b", b=P)[:, 0:2, :]).then_inc(s["am_ready"], 1)
            for j in range(3):
                mixed(2 * j, Y[:, j // 2, (j % 2) * 512:(j % 2 + 1) * 512])
            attention(PN1, False)
            mixed(6, Y[:, 0, 0:512])
            mixer_out()
            layer_norm(8, 24)
            moe(1)
            layer_norm(40, 56, xt=False)
            for t in range(NT):
                dve.wait_ge(s["x_ready"], n.at("xr"))
                dve.tensor_scalar(X[:, t, :], X[:, t, :], 1.0, None, ALU.mult).then_inc(s["x_sum"], 1)
            rms(70, ahead=False)
            dve.wait_ge(s["pos_in"], 16)
            a_, k_, r_ = SM[:, 384:416], SM[:, 416:480], SM[:, 320:384]
            after(dve.tensor_copy(SM[:, 480:482], POS[:, :]))
            for t in range(NT):
                did(dve.tensor_scalar(a_[:, t * 16:(t + 1) * 16], INVF[:, :], SM[:, 480 + t:481 + t], None, ALU.mult))
            dve.wait_ge(s["dve_chain"], n.at("dve_chain"))
            turn = 2 * np.pi
            magic = 1.5 * 2 ** 23
            did(dve.tensor_scalar(k_[:, 0:32], a_, float(1 / turn), None, ALU.mult))
            after(dve.tensor_scalar(k_[:, 32:64], a_, float(1 / turn), 0.25, ALU.mult, ALU.add))
            after(dve.tensor_scalar(k_, k_, magic, None, ALU.add))
            after(dve.tensor_scalar(k_, k_, -magic, None, ALU.add))
            c1 = 6.28125
            c2 = float(np.floor((turn - c1) * 2 ** 20) / 2 ** 20)
            c3 = float(turn - c1 - c2)
            k2, r2 = (v.rearrange("p (a b) -> p a b", a=2) for v in (k_, r_))
            after(dve.scalar_tensor_tensor(out=r2, in0=k2, scalar=-c1, in1=bc(a_.unsqueeze(1), 2, 32), op0=ALU.mult, op1=ALU.add))
            after(dve.scalar_tensor_tensor(out=r_, in0=k_, scalar=-c2, in1=r_, op0=ALU.mult, op1=ALU.add))
            after(dve.scalar_tensor_tensor(out=r_, in0=k_, scalar=-c3, in1=r_, op0=ALU.mult, op1=ALU.add))
            after(dve.tensor_scalar(r_[:, 32:64], r_[:, 32:64], float(np.pi / 2), None, ALU.add))
            after(dve.tensor_scalar(r_, r_, 3.1415925, -3.1415925, ALU.min, ALU.max), "rope_cs")
            ffn(D_FF // UC, 0, False)
            residual(0.5)
            rms(70 + 16)
            for j in range(7):
                used()
                split()
            dve.wait_ge(s["cq_act"], 3 * NT)
            for k, w in enumerate((384, 256, 512)):
                v = SM[:, 300 + 2 * k:302 + 2 * k]
                ins = dve.tensor_scalar(v, v, 1.0 / w, RMS_EPS, ALU.mult, ALU.add)
                if k == 2:
                    ins.then_inc(s["n_dve"], 1)
                else:
                    did(ins)
            for j in range(2):
                b = (3, 0)[j]
                dve.wait_ge(s["sgw_tp"], j + 1)
                dve.tensor_tensor(SGWT[:, 4 * j:4 * j + 4, :], PB[:, b, :].rearrange("p (g t) -> p g t", t=P),
                                  bc(TRIL[:, :].unsqueeze(1), 4, P), ALU.mult).then_inc(p_free[b], 1)
            dve.wait_ge(s["n_act"], n.next("na"))
            after(dve.reciprocal(SM[:, 306:312], SM[:, 300:306]))
            for k, (lo, hi) in enumerate(((0, 384), (384, 640))):
                for t in range(NT):
                    dve.tensor_scalar(PRJ[:, t, lo:hi], PRJ[:, t, lo:hi], SM[:, 306 + 2 * k + t:307 + 2 * k + t], None,
                                      ALU.mult).then_inc(s["cq_done"], 1)
            scaled(70 + 72, None, CTH, CTL, banks=((1, 0, 2), (2, 2, 2), (3, 4, 1)))
            dve.wait_ge(s["sgn_in"], 16)
            for t in range(NT):
                v = ZG[:, t, 512:1024]
                dve.scalar_tensor_tensor(out=v, in0=v, scalar=SM[:, 310 + t:311 + t], in1=LNB[:, 0:512],
                                         op0=ALU.mult, op1=ALU.mult).then_inc(s["vn_ready"], 1)
            dve.wait_ge(s["rope_act"], 1)
            sn = SM[:, 320:352].rearrange("p (t r) -> p t r", t=NT)
            cs = SM[:, 352:384].rearrange("p (t r) -> p t r", t=NT)

            def rope(t1, t2, w1, w2, w3, w4, bcast):
                for out_, x, y in ((w1, t1, cs), (w2, t2, sn), (w3, t1, sn), (w4, t2, cs)):
                    did(dve.tensor_tensor(out_, x, bcast(y), ALU.mult))
                dve.wait_ge(s["dve_chain"], n.at("dve_chain"))
                did(dve.tensor_tensor(t1, w1, w2, ALU.subtract))
                return dve.tensor_tensor(t2, w3, w4, ALU.add)

            kr = PRJ[:, :, 640:672]
            kw = [SM[:, 384 + 32 * k:416 + 32 * k].rearrange("p (t r) -> p t r", t=NT) for k in range(4)]
            after(rope(kr[:, :, 0:16], kr[:, :, 16:32], *kw, lambda y: y))
            kfr = KF.rearrange("p t (h c) -> p t h c", c=QKH)[:, :, :, NOPE:QKH]
            dve.tensor_copy(kfr, kr.unsqueeze(2).broadcast_to([P, NT, HEADS_MLA, ROPE])).then_inc(s["q_ev"], 1)
            for j in range(3):
                used()
                split()
            qr = QN.rearrange("p t (h c) -> p t h c", c=QKH)
            qw = [(SG, HT)[k // 2][:, (k % 2) * S:(k % 2 + 1) * S].rearrange("p (t h r) -> p t h r", t=NT, h=HEADS_MLA) for k in range(4)]
            rope(qr[:, :, :, 64:80], qr[:, :, :, 80:96], *qw,
                 lambda y: y.unsqueeze(2).broadcast_to([P, NT, HEADS_MLA, 16])).then_inc(s["q_ev"], 1)
            for j in range(4):
                used()
                split()
            dve.wait_ge(s["mix_full"], 1)
            for g in range(8):
                u = ZG[:, :, g * 64:(g + 1) * 64]
                ins = dve.scalar_tensor_tensor(out=u, in0=Y[:, 1, g * P:(g + 1) * P].rearrange("p (n c) -> p n c", n=NT),
                                               scalar=PV[:, 147 + g:148 + g], in1=u, op0=ALU.add, op1=ALU.mult)
                if g == 7:
                    ins.then_inc(s["sgo_ready"], 1)
            attention(PN2, True)
            attention(PN2, True)
            for j in range(2):
                mixed(2 * j, Y[:, 0, j * 512:(j + 1) * 512])
            for b in range(2):
                n.next("tp")
                mixed(4 + 2 * b, PB[:, b, :])
            mixer_out()
            residual(1.0)
            rms(70 + 32)
            ffn(D_FF // UC, 0, False)
            residual(0.5)
            rms(70 + 8)
            ffn(D_FF // UC, 0, False)
            residual(0.5)
            rms(70 + 24)
            did(dve.memset(CZ[0][:, :, 0:2], 0.0))
            after(dve.memset(CZ[1][:, :, 0:2], 0.0))
            for j in range(4):
                used()
                split()
                used()
                cz, cv = CZ[j % 2], CV[j % 2]
                b = (3 * j + 1) % 4
                dve.tensor_tensor(cz[:, :, 2:2 + S], CSB[j % 2][:, :, :], PB[:, b, :].rearrange("p (h t) -> p h t", h=2),
                                  ALU.mult).then_inc(p_free[b], 1)
                split()
                dve.wait_ge(s["w_split"], n.u)
                for tap in range(3):
                    for h in range(2):
                        w = PV[:, 70 + 48 + 8 * tap + 2 * j + h:70 + 49 + 8 * tap + 2 * j + h]
                        if tap == 0:
                            did(dve.tensor_scalar(cv[:, h, :], cz[:, h, 0:S], w, None, ALU.mult))
                        else:
                            did(dve.scalar_tensor_tensor(out=cv[:, h, :], in0=cz[:, h, tap:tap + S], scalar=w,
                                                         in1=cv[:, h, :], op0=ALU.mult, op1=ALU.add))
                    dve.wait_ge(s["dve_chain"], n.at("dve_chain"))
                used()
                b = (3 * j + 2) % 4
                dve.tensor_tensor(cv, cv, PB[:, b, :].rearrange("p (h t) -> p h t", h=2), ALU.mult)\
                    .then_inc(s["conv_done"], 1)
                mixed(2 * j, cv[:, :, :])
                split()
            mixer_out()
            residual(1.0)
            rms(70 + 40)
            ffn(D_FF // UC, 1, False)
            residual(0.5)
            dve.wait_ge(s["sq_sum"], n.next("sqs", NT))
            rooted(1.0 / D, RMS_EPS)
            dve.wait_ge(s["fin_in"], 16)
            for t in range(NT):
                dve.scalar_tensor_tensor(out=XN[:, t, :], in0=X[:, t, :], scalar=ST[:, t, 15:16], in1=LNG[:, :],
                                         op0=ALU.mult, op1=ALU.mult).then_inc(s["out_in"], 1)
            assert n.u == n.v == STREAM_UNITS, (n.u, n.v)

        @block.gpsimd
        def _(pool):
            c = [0]

            def after(ins):
                c[0] += 1
                ins.then_inc(s["pool_chain"], 1)
                pool.wait_ge(s["pool_chain"], c[0])

            def select(dst, op, base, pattern, mult, fill=0.0):
                return pool.affine_select(out=dst, in_=dst, compare_op=op, fill=fill, base=base, pattern=pattern,
                                          channel_multiplier=mult)

            for t, v in ((IDENT, 0.0), (ONES, 1.0), (STRICT, 1.0), (TRIL, 1.0), (NSUF, -1.0), (NONE, -1.0), (CAUS, 0.0)):
                after(pool.memset(t[:, :], v))
            for k, v in ((0, 1.0), (1, 0.0), (2, RMS_EPS)):
                after(pool.memset(COLS[:, k:k + 1], v))
            for k in range(4):
                after(pool.memset(W4[:, k:k + 1], 4.0 - k))
            inv = (10000.0 ** (-np.arange(0, ROPE, 2, dtype=np.float32) / np.float32(ROPE))).astype(np.float32)
            for k in range(ROPE // 2):
                after(pool.memset(INVF[:, k:k + 1], float(inv[k])))
            after(select(IDENT[:, :], ALU.not_equal, 0, [[-1, P]], 1, 1.0))
            after(select(STRICT[:, :], ALU.is_gt, 0, [[1, P]], -1))
            after(select(TRIL[:, :], ALU.is_ge, 0, [[1, P]], -1))
            after(select(NSUF[:, :], ALU.is_ge, 0, [[-1, P]], 1))
            select(CAUS[:, :], ALU.is_ge, 0, [[-1, P]], 1, NEG).then_inc(s["pool_const"], 1)
            lns = [("ln_mix_g", "ln_mix_b", 0), ("ln_ffn_g", "ln_ffn_b", 0), ("ln_mix_g", "ln_mix_b", 1), ("ln_ffn_g", "ln_ffn_b", 1)]

            def load_norm(k):
                g, b, layer = lns[k]
                pool.dma_start(LNG[:, :], a[g][layer].partition_broadcast(P)).then_inc(s["ln_in"], 16)
                pool.dma_start(LNB[:, :], a[b][layer].partition_broadcast(P)).then_inc(s["ln_in"], 16)

            load_norm(0)
            pool.dma_start(POS[:, :], a["positions_2"][0].rearrange("(t p) -> p t", p=P), allow_slow_non_contiguous=True)\
                .then_inc(s["pos_in"], 16)
            for k, B in enumerate(LEVELS):
                after(pool.memset(MTMP[:, :], 1.0))
                after(select(MTMP[:, :], ALU.is_ge, 0, [[-B, P // B], [0, B]], 1))
                after(select(MTMP[:, :], ALU.is_ge, B // 2 - 1, [[B, P // B], [0, B]], -1))
                after(pool.tensor_copy(MSK[:, k, :], MTMP[:, :]))
            after(pool.tensor_copy(MSK[:, 7, :], IDENT[:, :]))
            after(pool.tensor_copy(MSK[:, 8, :], STRICT[:, :]))
            pool.memset(ATD[:, :, :], 0.0).then_inc(s["at_ready"], 1)

            def halves(v, B):
                x = v.rearrange("p (n b) -> p n b", b=B)
                return x[:, :, 0:B // 2], x[:, :, B // 2:B]

            def decay_low(m):
                if m >= 4:
                    pool.wait_ge(s["lvl_full"], m - 1)
                B = LEVELS[m - 2] if m < 9 else S
                low = halves(G, B)[0]
                pool.tensor_tensor(halves(MB[m % 2], B)[0], low[:, :, B // 2 - 1:B // 2].broadcast_to([P, 1536 // B, B // 2]),
                                   low, ALU.subtract).then_inc(s["dlow"], 1)

            pool.wait_ge(s["q_ready"], 1)
            decay_low(2)
            for m in range(2, 10):
                if m < 9:
                    decay_low(m + 1)
                pool.wait_ge(s["e_done"], m - 1)
                B = LEVELS[m - 2] if m < 9 else S
                low = halves(MB[m % 2], B)[0]
                pool.tensor_tensor(low, low, halves(KK, B)[0], ALU.mult).then_inc(s["m_low"], 1)

            def norm(k):
                pool.wait_ge(s["xn_ready"], 2 * (k + 1))
                pool.wait_ge(s["ln_in"], 32 * (k + 1))
                for t in range(NT):
                    after(pool.tensor_tensor(X[:, t, :], XN[:, t, :], LNG[:, :], ALU.mult))
                    pool.tensor_tensor(X[:, t, :], X[:, t, :], LNB[:, :], ALU.add).then_inc(s["x_ready"], 1)
                pool.wait_ge(s["x_ready"], 2 * (k + 1))
                if k + 1 < len(lns):
                    load_norm(k + 1)

            def gates(layer):
                pool.wait_ge(s["gt_sb"], layer + 1)
                pool.dma_start(gate_dram[layer], SM[0:EXPERTS, 384:640]).then_inc(s["gt_out"], 16)
                pool.wait_ge(s["gt_out"], 16 * (layer + 1))
                pool.dma_start(GB.rearrange("p e t -> p (e t)"),
                               gate_dram[layer].rearrange("e t -> (e t)").partition_broadcast(P)).then_inc(s["gb_in"], 16)

            norm(0)
            gates(0)
            norm(1)
            pool.wait_ge(s["w_used"], 21 + 48)
            for z in range(2):
                ins = pool.memset(SBW[z][3], 0.0)
                if z:
                    ins.then_inc(s["am_zero"], 1)
                else:
                    after(ins)
            norm(2)
            gates(1)
            norm(3)
            pool.dma_start(LNG[:, :], a["final_norm_2"].partition_broadcast(P)).then_inc(s["fin_in"], 16)
            pool.dma_start(LNB[:, 0:512], a["sg_norm_2"][0].partition_broadcast(P)).then_inc(s["sgn_in"], 16)
            pool.wait_ge(s["w_used"], EVEN_UNIT - 33)
            pool.dma_start(SGW[:, :, :], a["sg_w_2"][0].rearrange("g t s -> t g s")).then_inc(s["sgw_in"], 16)
            pool.wait_ge(s["sgw_in"], 16)


_INS = ["x", "mem", "a_w_in", "a_lower_bounds", "a_gnorm", "b_w_in", "w_kv_shared", "w_mem_kv", "w_o", "ln_mix_g",
        "ln_mix_b", "ln_ffn_g", "ln_ffn_b", "w_group", "b_group", "w_router", "b_router", "w_gate", "w_up", "w_down",
        "positions_2", "ffn_pre_norm_2", "ffn_pre_w_gate_2", "ffn_pre_w_up_2", "ffn_pre_w_down_2", "mix_norm_2",
        "ffn_post_norm_2", "ffn_post_w_gate_2", "ffn_post_w_up_2", "ffn_post_w_down_2", "even_w_in_2", "q_norm_2",
        "w_uq_2", "kv_norm_2", "w_ukv_2", "sg_norm_2", "sg_w_2", "sg_b_2", "even_w_out_2", "conv_w_in_2", "conv_w_2",
        "conv_w_out_2", "final_norm_2"]


def kernel(**inputs):
    import numpy as _np
    import concourse.bacc as _bacc
    from concourse import mybir as _mybir
    from concourse.bass_utils import run_bass_kernel_spmd as _run

    nc = _bacc.Bacc("TRN2", target_bir_lowering=False, num_devices=1)
    arrays, args = {}, {}
    for name in _INS:
        arr = _np.ascontiguousarray(inputs[name])
        arrays[f"in_{name}"] = arr
        args[name] = nc.dram_tensor(f"in_{name}", arr.shape, _mybir.dt.from_np(arr.dtype), kind="ExternalInput").ap()
    out = nc.dram_tensor("out_0", (1, S, D), F32, kind="ExternalOutput").ap()
    build_kernel(nc, args, out)
    r = _run(nc, [arrays], core_ids=[0])
    return r.results[0]["out_0"]
```
